# Optimizing a Trainium2 kernel written in Bass

```python
import jax, jax.numpy as jnp
from jax import lax
import numpy as np

D_MODEL = 1024
BATCH = 1
SEQ = 1024
DEPTH = 1

CHUNK = 64
Q_BLOCK = 128
EPS = 1e-6

GLA_HEADS = 4
GLA_DK = 64
GLA_DV = 128
GLA_RANK = 16
GLA_TAU = 16.0
SB_HEADS = 8
SB_DH = 64
MEM_LEN = 256
MEM_HEADS = 4
MEM_DH = D_MODEL // MEM_HEADS
PEER_HEADS = 8
PEER_NKEYS = 128
PEER_N = PEER_NKEYS * PEER_NKEYS
PEER_DQ = 256
PEER_TOPK = 16
PEER_TOK_BLOCK = 128

GLA_QK = GLA_HEADS * GLA_DK
GLA_V = GLA_HEADS * GLA_DV
SB_W = SB_HEADS * SB_DH
MIX_W = GLA_V + SB_W
_SPLIT_SIZES = (GLA_QK, GLA_QK, GLA_V, GLA_V, GLA_RANK, SB_W, SB_W, SB_W)
IN_COLS = sum(_SPLIT_SIZES)

kernel_name = "hybrid_gla_stickbreak_peer_block"

def _rmsnorm(x, g):
    xf = x.astype(jnp.float32)
    y = xf * lax.rsqrt(jnp.mean(xf * xf, axis=-1, keepdims=True) + EPS)
    return (y * g.astype(jnp.float32)).astype(x.dtype)

def _gla(q, k, v, g):
    B_, S_, H, dk = q.shape
    dv = v.shape[-1]
    n = S_ // CHUNK

    def to_chunks(t):
        return t.reshape(B_, n, CHUNK, H, t.shape[-1]).transpose(1, 0, 3, 2, 4)

    qc, kc, vc, gc = (to_chunks(t) for t in (q * (dk ** -0.5), k, v, g))
    causal = jnp.tril(jnp.ones((CHUNK, CHUNK), dtype=bool))

    def step(state, inp):
        q_, k_, v_, g_ = inp
        b = jnp.cumsum(g_.astype(jnp.float32), axis=-2)
        b_last = b[..., -1:, :]
        o_inter = jnp.einsum('bhcd,bhde->bhce', q_ * jnp.exp(b), state)
        diff = b[:, :, :, None, :] - b[:, :, None, :, :]
        decay = jnp.where(causal[:, :, None], jnp.exp(jnp.minimum(diff, 0.0)), 0.0)
        attn = jnp.einsum('bhtd,bhsd,bhtsd->bhts', q_, k_, decay)
        o = o_inter + jnp.einsum('bhts,bhse->bhte', attn, v_)
        new_state = state * jnp.exp(b_last).swapaxes(-1, -2) + jnp.einsum(
            'bhsd,bhse->bhde', k_ * jnp.exp(b_last - b), v_)
        return new_state, o

    state0 = jnp.zeros((B_, H, dk, dv), jnp.float32)
    _, o = lax.scan(step, state0, (qc, kc, vc, gc))
    return o.transpose(1, 0, 3, 2, 4).reshape(B_, S_, H, dv)

def _stick_breaking(q, k, v):
    B_, S_, H, d = q.shape
    qh = q.transpose(0, 2, 1, 3).astype(jnp.float32) * (d ** -0.5)
    kh = k.transpose(0, 2, 1, 3).astype(jnp.float32)
    vh = v.transpose(0, 2, 1, 3).astype(jnp.float32)
    outs = []
    for i in range(S_ // Q_BLOCK):
        start, end = i * Q_BLOCK, (i + 1) * Q_BLOCK
        z = jnp.einsum('bhtd,bhsd->bhts', qh[:, :, start:end], kh[:, :, :end])
        mask = jnp.arange(end)[None, :] < jnp.arange(start, end)[:, None]
        log_1m = jnp.where(mask, jax.nn.log_sigmoid(-z), 0.0)
        suffix = lax.cumsum(log_1m, axis=3, reverse=True) - log_1m
        a = jnp.where(mask, jnp.exp(jax.nn.log_sigmoid(z) + suffix), 0.0)
        outs.append(jnp.einsum('bhts,bhsd->bhtd', a, vh[:, :, :end]))
    o = jnp.concatenate(outs, axis=2)
    return o.transpose(0, 2, 1, 3)

def _mem_xattn(hn, memn, w_q, w_kv, w_o):
    B_, S_, D = hn.shape
    M = memn.shape[1]
    q = (hn @ w_q).reshape(B_, S_, MEM_HEADS, MEM_DH)
    k, v = jnp.split(memn @ w_kv, 2, axis=-1)
    k = k.reshape(B_, M, MEM_HEADS, MEM_DH)
    v = v.reshape(B_, M, MEM_HEADS, MEM_DH)
    s = jnp.einsum('bshd,bmhd->bhsm', q, k).astype(jnp.float32) * (MEM_DH ** -0.5)
    p = jax.nn.softmax(s, axis=-1).astype(v.dtype)
    o = jnp.einsum('bhsm,bmhd->bshd', p, v).reshape(B_, S_, D)
    return o @ w_o

def _peer(xn, w_pq, sub_keys, u, v_emb):
    B_, S_, D = xn.shape
    T = B_ * S_
    H, K = PEER_HEADS, PEER_TOPK
    xt = xn.reshape(T, D)
    q = (xt @ w_pq).reshape(T, H, 2, PEER_DQ // 2)
    s = jnp.einsum('thpd,hpnd->thpn', q, sub_keys).astype(jnp.float32)
    top_s, top_i = lax.top_k(s, K)
    cand_s = top_s[:, :, 0, :, None] + top_s[:, :, 1, None, :]
    cand_i = top_i[:, :, 0, :, None] * PEER_NKEYS + top_i[:, :, 1, None, :]
    best_s, best_j = lax.top_k(cand_s.reshape(T, H, K * K), K)
    expert = jnp.take_along_axis(cand_i.reshape(T, H, K * K), best_j, axis=-1)
    gate = jax.nn.softmax(best_s, axis=-1)

    nb = T // PEER_TOK_BLOCK

    def block(args):
        xb, eb, gb = args
        ub = u[eb]
        act = jax.nn.gelu(jnp.einsum('thkd,td->thk', ub, xb).astype(jnp.float32),
                          approximate=False)
        w = (gb * act).astype(xb.dtype)
        return jnp.einsum('thk,thkd->td', w, v_emb[eb])

    out = lax.map(block, (xt.reshape(nb, PEER_TOK_BLOCK, D),
                          expert.reshape(nb, PEER_TOK_BLOCK, H, K),
                          gate.reshape(nb, PEER_TOK_BLOCK, H, K)))
    return out.reshape(B_, S_, D)

def setup_inputs(seed: int = 0) -> dict:
    key = jax.random.key(seed)
    ks = jax.random.split(key, 24)
    nrm = jax.random.normal
    f32 = jnp.float32
    L, D = DEPTH, D_MODEL

    def gain(k, shape):
        return 1.0 + 0.02 * nrm(k, shape, f32)

    return {
        "x": nrm(ks[0], (BATCH, SEQ, D), f32),
        "mem": nrm(ks[1], (BATCH, MEM_LEN, D), f32),
        "g_mix": gain(ks[2], (L, D)),
        "w_in": nrm(ks[3], (L, D, IN_COLS), f32) * D ** -0.5,
        "w_alpha_up": nrm(ks[4], (L, GLA_RANK, GLA_QK), f32) * GLA_RANK ** -0.5,
        "b_alpha": 0.1 * nrm(ks[5], (L, GLA_QK), f32),
        "g_gla_out": gain(ks[6], (L, GLA_DV)),
        "w_out": nrm(ks[7], (L, MIX_W, D), f32) * MIX_W ** -0.5,
        "g_mem_q": gain(ks[8], (L, D)),
        "g_mem_kv": gain(ks[9], (L, D)),
        "w_mq": nrm(ks[10], (L, D, D), f32) * D ** -0.5,
        "w_mkv": nrm(ks[11], (L, D, 2 * D), f32) * D ** -0.5,
        "w_mo": nrm(ks[12], (L, D, D), f32) * D ** -0.5,
        "g_ffn": gain(ks[13], (L, D)),
        "w_pq": nrm(ks[14], (L, D, PEER_HEADS * PEER_DQ), f32) * D ** -0.5,
        "sub_keys": nrm(ks[15], (L, PEER_HEADS, 2, PEER_NKEYS, PEER_DQ // 2), f32) * (PEER_DQ // 2) ** -0.5,
        "peer_u": nrm(ks[16], (L, PEER_N, D), f32) * D ** -0.5,
        "peer_v": nrm(ks[17], (L, PEER_N, D), f32) * (PEER_HEADS * PEER_TOPK) ** -0.5,
        "g_final": gain(ks[18], (D,)),
    }

def reference(x, mem, g_mix, w_in, w_alpha_up, b_alpha, g_gla_out, w_out,
              g_mem_q, g_mem_kv, w_mq, w_mkv, w_mo, g_ffn, w_pq, sub_keys,
              peer_u, peer_v, g_final):
    B_, S_, D = x.shape
    split_idx = np.cumsum(_SPLIT_SIZES)[:-1].tolist()
    h = x
    for i in range(DEPTH):
        hn = _rmsnorm(h, g_mix[i])
        proj = hn @ w_in[i]
        qg, kg, vg, og, alr, qs, ksb, vs = jnp.split(proj, split_idx, axis=-1)
        log_alpha = jax.nn.log_sigmoid(
            (alr @ w_alpha_up[i] + b_alpha[i]).astype(jnp.float32)) / GLA_TAU
        o_gla = _gla(qg.reshape(B_, S_, GLA_HEADS, GLA_DK),
                     kg.reshape(B_, S_, GLA_HEADS, GLA_DK),
                     vg.reshape(B_, S_, GLA_HEADS, GLA_DV),
                     log_alpha.reshape(B_, S_, GLA_HEADS, GLA_DK))
        o_gla = _rmsnorm(o_gla, g_gla_out[i]).reshape(B_, S_, GLA_V)
        o_gla = o_gla * jax.nn.silu(og.astype(jnp.float32))
        o_sb = _stick_breaking(qs.reshape(B_, S_, SB_HEADS, SB_DH),
                               ksb.reshape(B_, S_, SB_HEADS, SB_DH),
                               vs.reshape(B_, S_, SB_HEADS, SB_DH)).reshape(B_, S_, SB_W)
        mix = jnp.concatenate([o_gla, o_sb], axis=-1).astype(h.dtype)
        h = h + mix @ w_out[i]
        h = h + _mem_xattn(_rmsnorm(h, g_mem_q[i]), _rmsnorm(mem, g_mem_kv[i]),
                           w_mq[i], w_mkv[i], w_mo[i])
        h = h + _peer(_rmsnorm(h, g_ffn[i]), w_pq[i], sub_keys[i], peer_u[i], peer_v[i])
    return _rmsnorm(h, g_final)


_drawn_inputs = setup_inputs


def setup_inputs(seed=0):
    import zlib

    import numpy as np

    out = dict(_drawn_inputs(seed))
    spreads = {}
    factors = {'g_mix': 2.894,
     'b_alpha': 3.241,
     'g_gla_out': 6.735,
     'g_mem_q': 8.0,
     'g_mem_kv': 8.0,
     'g_ffn': 64.0,
     'g_final': 8.446}
    for name, (base, spread) in spreads.items():
        noise = np.random.default_rng([zlib.crc32(name.encode()), seed]).standard_normal(out[name].shape)
        drawn = base * np.exp(spread * noise) if base else spread * noise
        out[name] = __import__('jax').numpy.asarray(drawn.astype(out[name].dtype))
    for name, factor in factors.items():
        out[name] = (out[name] * factor).astype(out[name].dtype)
    return out
```

```python
from contextlib import ExitStack

import concourse.bass as bass
from concourse import mybir

F32 = mybir.dt.float32
U32 = mybir.dt.uint32
ALU = mybir.AluOpType
ACT = mybir.ActivationFunctionType
AX = mybir.AxisListType.X
ds = bass.ds

P = 128
SEQ = 1024
D = 1024
KT = D // P
NB = SEQ // P
HALF = 512
EPS = 1e-6

GLA_HEADS, GLA_DK, GLA_DV, RANK, TAU = 4, 64, 128, 16, 16.0
CHUNK = 64
SUB = 16
NSUB = CHUNK // SUB
SB_HEADS, SB_DH = 8, 64
MEM, MEM_HEADS, MEM_DH = 256, 4, 256
MB = MEM // P
PH, NKEYS, TOPK = 8, 128, 16
EXP_CAP = 80.0
LN_EXP = "natural_log_exp_and_others"

F_QG, F_KG, F_QS, F_KS, NFEAT = 0, 2, 4, 8, 12
T_VG, T_OG, T_VS, NTOK = 0, 1, 2, 3


class Chain:

    def __init__(self, eng, sem):
        self.eng, self.sem, self.n = eng, sem, 0

    def __call__(self, ins):
        self.n += 1
        ins.then_inc(self.sem, 1)
        self.eng.wait_ge(self.sem, self.n)

    def restart(self):
        self.eng.sem_clear(self.sem)
        self.n = 0


def wait_alone(co, eng, sem, value):
    eng.wait_ge(sem, value)
    eng.sem_inc(co.steps, 1)


class Core:

    def __init__(self, nc, ctx):
        self.nc, self.ctx = nc, ctx
        self.phase_sems, self.stale = [], []

    def sem(self, name):
        self.phase_sems.append(self.nc.alloc_semaphore(name=name))
        return self.phase_sems[-1]

    def end_phase(self):
        self.stale, self.phase_sems = self.phase_sems, []
        for s in self.stale:
            self.nc.release_semaphore(s)

    def clear_stale(self, pool):
        for s in self.stale:
            pool.sem_clear(s)

    def sb(self, name, shape, dt=F32, ctx=None):
        return (ctx or self.ctx).enter_context(self.nc.sbuf_tensor(name, shape, dt))


def steps(eng, first, second):
    first(0, 0)
    with eng.Fori(0, NB // 2 - 1) as i:
        first(2 * i + 1, 1)
        second(2 * i, 0)
        first(2 * i + 2, 0)
        second(2 * i + 1, 1)
    first(NB - 1, 1)
    second(NB - 2, 0)
    second(NB - 1, 1)


def rstd_steps(link, nc, ms, v, t, y):
    for _ in range(2):
        link(nc.vector.tensor_tensor(t, y, y, ALU.mult))
        link(nc.vector.tensor_tensor(t, t, v, ALU.mult))
        link(nc.vector.tensor_scalar(t, t, -0.5, 1.5, ALU.mult, ALU.add))
        link(nc.vector.tensor_tensor(y, y, t, ALU.mult))


def norm_phase(co, name, tok, nb, gain, feat, rstd, loads=()):
    nc = co.nc
    sem = lambda n: co.sem(f"{name}_{n}")
    landed = [sem(f"landed{i}") for i in range(len(loads))]
    sums_a, sums_v, var_ready, guess_ready = sem("sums_a"), sem("sums_v"), sem("var_ready"), sem("guess_ready")
    scaled, turned, act_done = sem("scaled"), sem("turned"), sem("act_done")
    vlink_s = sem("vlink")
    per = nb // max(1, len(loads))
    with ExitStack() as cx:
        ms = co.sb(f"{name}_ms", [P, nb], ctx=cx)
        var = co.sb(f"{name}_var", [P, nb], ctx=cx)
        tmp = co.sb(f"{name}_tmp", [P, nb], ctx=cx)
        xs = co.sb(f"{name}_xs", [P, 2, D], ctx=cx)
        pt = [cx.enter_context(nc.psum_tensor(f"{name}_pt{j}", [P, KT, P], F32)) for j in range(2)]
        junk = [cx.enter_context(nc.psum_tensor(f"{name}_junk{j}", [P, D], F32)) for j in range(2)]
        block = cx.enter_context(nc.Block())

        @block.gpsimd
        def _(pool):
            co.clear_stale(pool)

        @block.sync
        def _(sp):
            for s, (dst, src) in zip(landed, loads):
                sp.dma_start(dst, src).then_inc(s, 16)

        @block.scalar
        def _(act):
            act.preload_act_table_set(LN_EXP)
            link = Chain(act, act_done)
            for b in range(0, nb, 2):
                if loads:
                    act.wait_ge(landed[b // per], 16)
                link(nc.scalar.activation(junk[0][:, :], tok[:, b, :], ACT.Square, accum_out=ms[:, b:b + 1]))
            act.sem_inc(sums_a, 1)
            act.wait_ge(var_ready, 1)
            link(nc.scalar.activation(tmp[:, :], var[:, :], ACT.Ln))
            nc.scalar.activation(rstd, tmp[:, :], ACT.Exp, scale=-0.5).then_inc(guess_ready, 1)

        @block.vector
        def _(dve):
            link = Chain(dve, vlink_s)
            for b in range(1, nb, 2):
                if loads:
                    dve.wait_ge(landed[b // per], 16)
                link(nc.vector.tensor_tensor_reduce(junk[1][:, :], tok[:, b, :], tok[:, b, :], 1.0, 0.0,
                                                    ALU.mult, ALU.add, ms[:, b:b + 1]))
            dve.wait_ge(sums_a, 1)
            nc.vector.tensor_scalar(var[:, :], ms[:, :], 1.0 / D, EPS, ALU.mult, ALU.add).then_inc(var_ready, 1)
            dve.wait_ge(guess_ready, 1)
            rstd_steps(link, nc, ms[:, :], var[:, :], tmp[:, :], rstd)
            with dve.Fori(0, nb // 2) as i:
                link.restart()
                for j in range(2):
                    nc.vector.tensor_scalar(xs[:, j, :], tok[:, ds(2 * i + j, 1), :].rearrange("p o d -> p (o d)"),
                                            rstd[:, ds(2 * i + j, 1)], None, ALU.mult).then_inc(scaled, 1)
                for j in range(2):
                    dve.wait_ge(turned, 2 * i + j + 1)
                    link(nc.vector.tensor_tensor(feat[:, :, ds((2 * i + j) * P, P)], pt[j][:, :, :],
                                                 gain.unsqueeze(2).broadcast_to([P, KT, P]), ALU.mult))

        @block.tensor
        def _(pe):
            with pe.Fori(0, nb // 2) as i:
                for j in range(2):
                    pe.wait_ge(scaled, 2 * i + j + 1)
                    for k in range(KT):
                        last = nc.tensor.transpose(pt[j][:, k, :], xs[:, j, k * P:(k + 1) * P], co.ident[:, :])
                    last.then_inc(turned, 1)
    co.end_phase()


def feature_gemm_phase(co, name, act_t, width, weights, n_tiles, out, ctx_loads=()):
    nc = co.nc
    sem = lambda n: co.sem(f"{name}_{n}")
    U = 4
    step = min(width, HALF)
    parts = width // step
    landed = [sem(f"landed{j}") for j in range(U)]
    bank_full, bank_free = sem("bank_full"), sem("bank_free")
    with ExitStack() as cx:
        w = [co.sb(f"{name}_w{j}", [P, KT, P], ctx=cx) for j in range(U)]
        banks = [cx.enter_context(nc.psum_tensor(f"{name}_bank{j}", [P, HALF], F32)) for j in range(U * parts)]
        block = cx.enter_context(nc.Block())

        @block.gpsimd
        def _(pool):
            co.clear_stale(pool)

        @block.sync
        def _(sp):
            for j in range(U):
                sp.dma_start(w[j][:, :, :].rearrange("p k c -> p (k c)"), weights[j]).then_inc(landed[j], 16)
            with sp.Fori(0, n_tiles // U - 1) as i:
                for j in range(U):
                    sp.wait_ge(bank_full, parts * (U * i + j + 1))
                    sp.dma_start(w[j][:, :, :].rearrange("p k c -> p (k c)"),
                                 weights[ds(U * i + U + j, 1)].rearrange("o p c -> p (o c)")).then_inc(landed[j], 16)

        @block.tensor
        def _(pe):
            with pe.Fori(0, n_tiles // U) as i:
                for j in range(U):
                    pe.wait_ge(landed[j], 16 * i + 16)
                    for h in range(parts):
                        pe.wait_ge(bank_free, U * parts * i + parts * j + h + 1)
                        for k in range(KT):
                            last = nc.tensor.matmul(banks[parts * j + h][:, 0:step], w[j][:, k, :],
                                                    act_t[:, k, h * step:(h + 1) * step],
                                                    start=(k == 0), stop=(k == KT - 1))
                        last.then_inc(bank_full, 1)

        @block.scalar
        def _(act):
            act.sem_inc(bank_free, U * parts)
            with act.Fori(0, n_tiles // U) as i:
                for j in range(U):
                    for h in range(parts):
                        act.wait_ge(bank_full, U * parts * i + parts * j + h + 1)
                        nc.scalar.activation(out[:, ds(U * i + j, 1), h * step:(h + 1) * step].rearrange("p o t -> p (o t)"),
                                             banks[parts * j + h][:, 0:step], ACT.Copy).then_inc(bank_free, 1)
    co.end_phase()


def token_gemm_phase(co, name, act_t, nb, weights, n_chunks, evac, loads=None):
    nc = co.nc
    sem = lambda n: co.sem(f"{name}_{n}")
    landed, bank_full, bank_free = sem("landed"), sem("bank_full"), sem("bank_free")
    loads = loads or []
    extra = [sem(f"extra{j}") for j in range(len(loads))]
    with ExitStack() as cx:
        w = co.sb(f"{name}_w", [P, 2, KT * HALF], ctx=cx)
        wv = w[:, :, :].rearrange("p s (k c) -> p s k c", k=KT)
        banks = [cx.enter_context(nc.psum_tensor(f"{name}_bank{j}", [P, HALF], F32)) for j in range(nb)]
        block = cx.enter_context(nc.Block())

        @block.gpsimd
        def _(pool):
            co.clear_stale(pool)

        @block.sync
        def _(sp):
            for c in range(n_chunks):
                if c >= 2:
                    sp.wait_ge(bank_full, nb * (c - 1))
                if c >= 1:
                    sp.wait_ge(landed, 16 * c)
                sp.dma_start(w[:, c % 2, :], weights[c]).then_inc(landed, 16)
                if c == 0:
                    for (dst, src), s in zip(loads, extra):
                        sp.dma_start(dst, src).then_inc(s, 16)

        @block.tensor
        def _(pe):
            with pe.Fori(0, n_chunks) as c:
                pe.wait_ge(landed, 16 * c + 16)
                for b in range(nb):
                    pe.wait_ge(bank_free, nb * c + b + 1)
                    for k in range(KT):
                        last = nc.tensor.matmul(banks[b][:, :], act_t[:, k, b * P:(b + 1) * P],
                                                wv[:, ds(c % 2, 1), k, :].rearrange("p o c -> p (o c)"),
                                                start=(k == 0), stop=(k == KT - 1))
                    last.then_inc(bank_full, 1)

        @block.vector
        def _(dve):
            dve.sem_inc(bank_free, nb)
            for s in extra:
                dve.wait_ge(s, 16)
            with dve.Fori(0, n_chunks) as c:
                for b in range(nb):
                    dve.wait_ge(bank_full, nb * c + b + 1)
                    evac(c, b, banks[b]).then_inc(bank_free, 1)
    co.end_phase()


def decay_phase(co, act_t, w_alr, w_up, b_alpha, decay):
    nc = co.nc
    sem = lambda n: co.sem(f"decay_{n}")
    loaded, rank_full, rank_ready, gate_full = sem("loaded"), sem("rank_full"), sem("rank_ready"), sem("gate_full")
    gate_ready, log_ready, reset_ready, done, act_done = (sem("gate_ready"), sem("log_ready"), sem("reset_ready"),
                                                         sem("done"), sem("act_done"))
    with ExitStack() as cx:
        wa = co.sb("decay_wa", [P, KT, RANK], ctx=cx)
        wu = co.sb("decay_wu", [RANK, 2 * P], ctx=cx)
        ba = co.sb("decay_ba", [P, 2], ctx=cx)
        rank_t = co.sb("decay_rank_t", [RANK, SEQ], ctx=cx)
        gate = co.sb("decay_gate", [P, 2, SEQ], ctx=cx)
        mag = co.sb("decay_mag", [P, 2, SEQ], ctx=cx)
        keep = co.sb("decay_keep", [P, SEQ], ctx=cx)
        pr = cx.enter_context(nc.psum_tensor("decay_pr", [RANK, SEQ], F32))
        pg = cx.enter_context(nc.psum_tensor("decay_pg", [P, 2, SEQ], F32))
        block = cx.enter_context(nc.Block())

        @block.sync
        def _(sp):
            for dst, src in ((wa[:, :, :], w_alr), (wu[:, :], w_up), (ba[:, :], b_alpha)):
                sp.dma_start(dst, src).then_inc(loaded, 16)

        @block.gpsimd
        def _(pool):
            co.clear_stale(pool)
            pool.memset(keep[:, :], 1.0).then_inc(reset_ready, 1)
            pool.wait_ge(reset_ready, 1)
            pool.memset(keep[:, :].rearrange("p (c t) -> p c t", t=CHUNK)[:, :, 0:1], 0.0).then_inc(reset_ready, 1)

        @block.tensor
        def _(pe):
            pe.wait_ge(loaded, 48)
            for h in range(2):
                for k in range(KT):
                    last = nc.tensor.matmul(pr[:, h * HALF:(h + 1) * HALF], wa[:, k, :],
                                            act_t[:, k, h * HALF:(h + 1) * HALF], start=(k == 0), stop=(k == KT - 1))
                last.then_inc(rank_full, 1)
            for h in range(2):
                pe.wait_ge(rank_ready, h + 1)
                for p in range(2):
                    last = nc.tensor.matmul(pg[:, p, h * HALF:(h + 1) * HALF], wu[:, p * P:(p + 1) * P],
                                            rank_t[:, h * HALF:(h + 1) * HALF], start=True, stop=True)
            last.then_inc(gate_full, 1)

        @block.scalar
        def _(act):
            act.preload_act_table_set(LN_EXP)
            link = Chain(act, act_done)
            for h in range(2):
                act.wait_ge(rank_full, h + 1)
                nc.scalar.activation(rank_t[:, h * HALF:(h + 1) * HALF], pr[:, h * HALF:(h + 1) * HALF],
                                     ACT.Copy).then_inc(rank_ready, 1)
            for p in range(2):
                act.wait_ge(gate_ready, p + 1)
                link(nc.scalar.activation(mag[:, p, :], gate[:, p, :], ACT.Abs))
                link(nc.scalar.activation(mag[:, p, :], mag[:, p, :], ACT.Exp, scale=-1.0))
                nc.scalar.activation(mag[:, p, :], mag[:, p, :], ACT.Ln, bias=1.0).then_inc(log_ready, 1)

        @block.vector
        def _(dve):
            link = Chain(dve, done)
            dve.wait_ge(gate_full, 1)
            dve.wait_ge(loaded, 48)
            for p in range(2):
                link(nc.vector.tensor_scalar(gate[:, p, :], pg[:, p, :], ba[:, p:p + 1], None, ALU.add))
                dve.sem_inc(gate_ready, 1)
            for p in range(2):
                dve.wait_ge(log_ready, p + 1)
                link(nc.vector.scalar_tensor_tensor(gate[:, p, :], gate[:, p, :], 0.0, mag[:, p, :],
                                                    ALU.min, ALU.subtract))
                dve.wait_ge(reset_ready, 2)
                link(nc.vector.tensor_tensor_scan(decay[:, p, :], keep[:, :], gate[:, p, :], 0.0, ALU.mult, ALU.add))
    co.end_phase()


def gla_phase(co, feat, tok, decay):
    nc = co.nc
    sem = lambda n: co.sem(f"gla_{n}")
    args, exps, operands, values = sem("args"), sem("exps"), sem("operands"), sem("values")
    scores, turned, turned_sb, masked = sem("scores"), sem("turned"), sem("turned_sb"), sem("masked")
    sums, state_ready, o_full, o_free = sem("sums"), sem("state_ready"), sem("o_full"), sem("o_free")
    done, act_done, consts = sem("done"), sem("act_done"), sem("consts")
    NC = P // CHUNK
    with ExitStack() as cx:
        eq = co.sb("gla_eq", [P, 2, P], ctx=cx)
        ei = co.sb("gla_ei", [P, 2, P], ctx=cx)
        ek = co.sb("gla_ek", [P, 2, NC, NSUB, CHUNK], ctx=cx)
        ed = co.sb("gla_ed", [P, 2, P], ctx=cx)
        end = co.sb("gla_end", [P, 2, 2, NC], ctx=cx)
        qh = co.sb("gla_qh", [P, 2, 2, P], ctx=cx)
        qi = co.sb("gla_qi", [P, 2, 2, P], ctx=cx)
        kh = co.sb("gla_kh", [P, 2, 2, NC, NSUB, CHUNK], ctx=cx)
        kd = co.sb("gla_kd", [P, 2, 2, P], ctx=cx)
        kt = co.sb("gla_kt", [P, 2, 2 * P], ctx=cx)
        at = co.sb("gla_at", [P, 2, GLA_HEADS, P], ctx=cx)
        vb = co.sb("gla_vb", [P, 2, HALF], ctx=cx)
        state = co.sb("gla_state", [P, 2, 2, GLA_DV], ctx=cx)
        mask = co.sb("gla_mask", [P, 2, CHUNK], ctx=cx)
        ps = lambda n, shape: cx.enter_context(nc.psum_tensor(n, shape, F32))
        pa = [ps(f"gla_pa{j}", [P, 2, CHUNK]) for j in range(2)]
        po = [ps(f"gla_po{j}", [P, 2, GLA_DV]) for j in range(2)]
        pst = [ps(f"gla_pst{j}", [P, 2, GLA_DV]) for j in range(2)]
        pk = ps("gla_pk", [P, 2 * P])
        block = cx.enter_context(nc.Block())

        def blk(ap, b):
            return ap[:, :, ds(b * P, P)]

        @block.gpsimd
        def _(pool):
            co.clear_stale(pool)
            pool.memset(state[:, :, :, :], 0.0).then_inc(state_ready, 1)
            pool.memset(at[:, :, :, :], 0.0).then_inc(consts, 1)
            pool.memset(mask[:, :, :], 1.0).then_inc(consts, 1)
            pool.wait_ge(consts, 2)
            pool.affine_select(out=mask[:, :, :], in_=mask[:, :, :], compare_op=ALU.is_ge, fill=0.0, base=0,
                               pattern=[[CHUNK, 2], [1, CHUNK]], channel_multiplier=-1).then_inc(consts, 1)

            def value(b, s):
                pool.tensor_copy(vb[:, s, :], tok[:, T_VG, ds(b, 1), :].rearrange("p o c -> p (o c)")).then_inc(values, 1)

            value(0, 0)
            value(1, 1)
            with pool.Fori(0, NB // 2 - 1) as i:
                for s in range(2):
                    pool.wait_ge(sums, 2 * (2 * i + s + 1))
                    value(2 * i + 2 + s, s)

        @block.vector
        def _(dve):
            link = Chain(dve, done)

            def operand(b, s):
                link.restart()
                bb = blk(decay, b)
                mid = bb.rearrange("p a (u s) -> p a u s", s=SUB)
                nc.vector.tensor_tensor(eq[:, :, :].rearrange("p a (u s) -> p a u s", s=SUB), mid,
                                        mid[:, :, :, SUB // 2 - 1:SUB // 2].broadcast_to([P, 2, P // SUB, SUB]),
                                        ALU.subtract).then_inc(args, 1)
                for a in range(2):
                    row = decay[:, a, ds(b * P, P)].rearrange("p (c t) -> p c t", c=NC)
                    ref = row.rearrange("p c (u s) -> p c u s", s=SUB)[:, :, :, SUB // 2 - 1:SUB // 2]
                    link(nc.vector.tensor_tensor(ek[:, a, :, :, :], ref.broadcast_to([P, NC, NSUB, CHUNK]),
                                                 row.unsqueeze(2).broadcast_to([P, NC, NSUB, CHUNK]), ALU.subtract))
                ekf = ek[:, :, :, :, :].rearrange("p a c u s -> p (a c u s)")
                nc.vector.tensor_scalar(ekf, ekf, EXP_CAP * TAU, None, ALU.min).then_inc(args, 1)
                row = bb.rearrange("p a (c t) -> p a c t", c=NC)
                nc.vector.tensor_tensor(ed[:, :, :].rearrange("p a (c t) -> p a c t", c=NC),
                                        row[:, :, :, CHUNK - 1:CHUNK].broadcast_to([P, 2, NC, CHUNK]), row,
                                        ALU.subtract).then_inc(args, 1)
                q, k = blk(feat[:, F_QG:F_QG + 2, :], b), blk(feat[:, F_KG:F_KG + 2, :], b)
                dve.wait_ge(exps, 4 * b + 2)
                nc.vector.scalar_tensor_tensor(qh[:, s, :, :], q, GLA_DK ** -0.5, eq[:, :, :], ALU.mult, ALU.mult)\
                    .then_inc(done, 1)
                nc.vector.scalar_tensor_tensor(qi[:, s, :, :], q, GLA_DK ** -0.5, ei[:, :, :], ALU.mult, ALU.mult)\
                    .then_inc(done, 1)
                dve.wait_ge(exps, 4 * b + 3)
                for a in range(2):
                    kk = feat[:, F_KG + a, ds(b * P, P)].rearrange("p (c t) -> p c t", c=NC)
                    nc.vector.tensor_tensor(kh[:, s, a, :, :, :], ek[:, a, :, :, :],
                                            kk.unsqueeze(2).broadcast_to([P, NC, NSUB, CHUNK]), ALU.mult).then_inc(done, 1)
                dve.wait_ge(exps, 4 * b + 4)
                link.n += 4
                link(nc.vector.tensor_tensor(kd[:, s, :, :], ed[:, :, :], k, ALU.mult))
                dve.sem_inc(operands, 1)

            def attend(b, s):
                link.restart()
                dve.wait_ge(scores, b + 1)
                dve.wait_ge(consts, 3)
                atv = at[:, s, :, :].rearrange("p (a h) t -> p a h t", h=2)
                for h in range(2):
                    for c in range(NC):
                        rows = slice(c * CHUNK, (c + 1) * CHUNK)
                        link(nc.vector.tensor_tensor(
                            atv[rows, :, h, c * CHUNK:(c + 1) * CHUNK], pa[h][rows, :, :],
                            mask[rows, c:c + 1, :].broadcast_to([CHUNK, 2, CHUNK]), ALU.mult))
                dve.sem_inc(masked, 1)
                for c in range(NC):
                    dve.wait_ge(sums, 2 * b + c + 1)
                    for a in range(2):
                        link(nc.vector.scalar_tensor_tensor(state[:, 1 - c, a, :], state[:, c, a, :],
                                                            end[:, s, a, c:c + 1], pst[c][:, a, :], ALU.mult, ALU.add))
                    dve.sem_inc(state_ready, 1)

            steps(dve, operand, attend)

        @block.scalar
        def _(act):
            def operand(b, s):
                act.wait_ge(args, 3 * b + 1)
                nc.scalar.activation(eq[:, :, :], eq[:, :, :], ACT.Exp, scale=1 / TAU).then_inc(exps, 1)
                nc.scalar.activation(ei[:, :, :], blk(decay, b), ACT.Exp, scale=1 / TAU).then_inc(exps, 1)
                act.wait_ge(args, 3 * b + 2)
                ekf = ek[:, :, :, :, :].rearrange("p a c u s -> p (a c u s)")
                nc.scalar.activation(ekf, ekf, ACT.Exp, scale=1 / TAU).then_inc(exps, 1)
                act.wait_ge(args, 3 * b + 3)
                row = blk(decay, b).rearrange("p a (c t) -> p a c t", c=NC)
                nc.scalar.activation(end[:, s, :, :], row[:, :, :, CHUNK - 1], ACT.Exp, scale=1 / TAU).then_inc(act_done, 1)
                act.wait_ge(act_done, b + 1)
                nc.scalar.activation(ed[:, :, :], ed[:, :, :], ACT.Exp, scale=1 / TAU).then_inc(exps, 1)

            def attend(b, s):
                act.wait_ge(turned, b + 1)
                nc.scalar.activation(kt[:, s, :], pk[:, :], ACT.Copy).then_inc(turned_sb, 1)
                act.wait_ge(o_full, b + 1)
                ov = tok[:, T_VG, ds(b, 1), :].rearrange("p o (a h e) -> p (o a) h e", a=2, h=2)
                for h in range(2):
                    nc.scalar.activation(ov[:, :, h, :], po[h][:, :, :], ACT.Copy).then_inc(o_free, 1)

            act.sem_inc(o_free, 2)
            steps(act, operand, attend)

        @block.tensor
        def _(pe):
            with pe.Fori(0, NB // 2) as i:
                for s in range(2):
                    b = 2 * i + s
                    wait_alone(co, pe, operands, b + 1)
                    for h in range(2):
                        feats = slice(h * CHUNK, (h + 1) * CHUNK)
                        for a in range(2):
                            for c in range(NC):
                                for u in range(NSUB):
                                    last = nc.tensor.matmul(
                                        pa[h][c * CHUNK:(c + 1) * CHUNK, a, u * SUB:(u + 1) * SUB],
                                        kh[feats, s, a, c, u, :],
                                        qh[feats, s, a, c * CHUNK + u * SUB:c * CHUNK + (u + 1) * SUB],
                                        start=True, stop=True)
                    last.then_inc(scores, 1)
                    for a in range(2):
                        last = nc.tensor.transpose(pk[:, a * P:(a + 1) * P], kd[:, s, a, :], co.ident[:, :])
                    last.then_inc(turned, 1)
                    pe.wait_ge(masked, b + 1)
                    pe.wait_ge(values, b + 1)
                    pe.wait_ge(o_free, 2 * b + 2)
                    for h in range(2):
                        for a in range(2):
                            nc.tensor.matmul(po[h][:, a, :], at[:, s, 2 * a + h, :],
                                             vb[:, s, (2 * a + h) * GLA_DV:(2 * a + h + 1) * GLA_DV],
                                             start=(a == 0), stop=False, skip_group_check=True)
                    for c in range(NC):
                        rows = slice(c * CHUNK, (c + 1) * CHUNK)
                        wait_alone(co, pe, state_ready, 2 * b + c + 1)
                        for h in range(2):
                            feats = slice(h * CHUNK, (h + 1) * CHUNK)
                            for a in range(2):
                                last = nc.tensor.matmul(po[h][rows, a, :], qi[feats, s, a, rows], state[feats, c, a, :],
                                                        start=False, stop=(c == NC - 1), skip_group_check=True)
                        if c == NC - 1:
                            last.then_inc(o_full, 1)
                        if c == 0:
                            wait_alone(co, pe, turned_sb, b + 1)
                        for h in range(2):
                            feats = slice(h * CHUNK, (h + 1) * CHUNK)
                            for a in range(2):
                                hd = 2 * a + h
                                last = nc.tensor.matmul(pst[c][feats, a, :], kt[rows, s, hd * GLA_DK:(hd + 1) * GLA_DK],
                                                        vb[rows, s, hd * GLA_DV:(hd + 1) * GLA_DV], start=True, stop=True)
                        last.then_inc(sums, 1)
    co.end_phase()


def gla_norm_phase(co, tok, gain, mix_t):
    nc = co.nc
    sem = lambda n: co.sem(f"glanorm_{n}")
    var_ready, guess_ready, gate_ready, scaled, turned, done, act_done, loaded, free = (
        sem("var_ready"), sem("guess_ready"), sem("gate_ready"), sem("scaled"), sem("turned"), sem("done"),
        sem("act_done"), sem("loaded"), sem("free"))
    R = NB * GLA_HEADS
    with ExitStack() as cx:
        small = co.sb("glanorm_small", [P, 4, R], ctx=cx)
        g = co.sb("glanorm_gain", [P, 1], ctx=cx)
        sq = co.sb("glanorm_sq", [P, NB, HALF], ctx=cx)
        pt = [cx.enter_context(nc.psum_tensor(f"glanorm_pt{j}", [P, GLA_HEADS, P], F32)) for j in range(2)]
        block = cx.enter_context(nc.Block())
        ms, var, tmp, rstd = (small[:, j, :] for j in range(4))
        o = tok[:, T_VG, :, :]
        gate = tok[:, T_OG, :, :]
        rows = lambda ap: ap.rearrange("p b (h e) -> p (b h) e", e=GLA_DV)

        @block.gpsimd
        def _(pool):
            co.clear_stale(pool)

        @block.sync
        def _(sp):
            sp.dma_start(g[:, :], gain).then_inc(loaded, 16)

        @block.vector
        def _(dve):
            link = Chain(dve, done)
            link(nc.vector.tensor_tensor(sq[:, :, :], o, o, ALU.mult))
            link(nc.vector.tensor_reduce(ms, rows(sq[:, :, :]), AX, ALU.add))
            nc.vector.tensor_scalar(var, ms, 1.0 / GLA_DV, EPS, ALU.mult, ALU.add).then_inc(var_ready, 1)
            dve.wait_ge(guess_ready, 1)
            rstd_steps(link, nc, ms, var, tmp, rstd)
            for b in range(NB):
                ob = tok[:, T_VG, b, :].rearrange("p (h e) -> p h e", e=GLA_DV)
                r = small[:, 3, b * GLA_HEADS:(b + 1) * GLA_HEADS].unsqueeze(2).broadcast_to([P, GLA_HEADS, GLA_DV])
                link(nc.vector.tensor_tensor(ob, ob, r, ALU.mult))
                dve.wait_ge(gate_ready, 1)
                nc.vector.tensor_tensor(ob, ob, tok[:, T_OG, b, :].rearrange("p (h e) -> p h e", e=GLA_DV),
                                        ALU.mult).then_inc(scaled, 1)

        @block.tensor
        def _(pe):
            for b in range(NB):
                pe.wait_ge(scaled, b + 1)
                if b >= 2:
                    pe.wait_ge(free, b - 1)
                for h in range(GLA_HEADS):
                    last = nc.tensor.transpose(pt[b % 2][:, h, :], tok[:, T_VG, b, h * P:(h + 1) * P], co.ident[:, :])
                last.then_inc(turned, 1)

        @block.scalar
        def _(act):
            act.preload_act_table_set(LN_EXP)
            link = Chain(act, act_done)
            act.wait_ge(var_ready, 1)
            link(nc.scalar.activation(tmp, var, ACT.Ln))
            nc.scalar.activation(rstd, tmp, ACT.Exp, scale=-0.5).then_inc(guess_ready, 1)
            nc.scalar.activation(gate, gate, ACT.Silu).then_inc(gate_ready, 1)
            act.wait_ge(loaded, 16)
            for b in range(NB):
                act.wait_ge(turned, b + 1)
                nc.scalar.activation(mix_t[:, 0:GLA_HEADS, b * P:(b + 1) * P], pt[b % 2][:, :, :], ACT.Copy,
                                     scale=g[:, 0:1]).then_inc(free, 1)
    co.end_phase()


def stick_phase(co, feat, tok, mix_t, negtri, negone):
    nc = co.nc
    sem = lambda n: co.sem(f"stick_{n}")
    z_full, logs, sp_ready, sp_masked, carry_ready, r_full, a_ready, a_masked, pv_done, o_free = (
        sem(n) for n in ("z_full", "logs", "sp_ready", "sp_masked", "carry_ready", "r_full", "a_ready",
                         "a_masked", "pv_done", "o_free"))
    q_ready, kv_ready, act_done = sem("q_ready"), sem("kv_ready"), sem("act_done")
    NH = SEQ // HALF
    QB = HALF // P
    S = 4

    work = [(h, th, j, max(0, j - QB * th) * P) for th in range(NH) for j in range(QB * th + QB - 1, -1, -1)
            for h in range(2)]
    N = len(work)
    diag = [j >= QB * th for _, th, j, _ in work]
    carries = [j > 0 for _, _, j, _ in work]
    last_of = [j == 0 for _, _, j, _ in work]
    adds = [0 if not c else (1 if not d else (2 if w[3] + P < HALF else 1)) for c, d, w in zip(carries, diag, work)]
    C = 2

    def upto(flags, n):
        return sum(flags[:n + 1]) if n >= -1 else -sum(flags[n + 1:])

    with ExitStack() as cx:
        qp = co.sb("stick_q", [P, SEQ], ctx=cx)
        kp = co.sb("stick_k", [P, SEQ], ctx=cx)
        vp = co.sb("stick_v", [P, NB, P], ctx=cx)
        t = co.sb("stick_t", [P, S, HALF], ctx=cx)
        sps = co.sb("stick_sp", [P, S, HALF], ctx=cx)
        aw = co.sb("stick_a", [P, S, HALF], ctx=cx)
        carry = co.sb("stick_carry", [P, 2, 2, HALF], ctx=cx)
        pz = [cx.enter_context(nc.psum_tensor(f"stick_pz{j}", [P, HALF], F32)) for j in range(S)]
        po = [[cx.enter_context(nc.psum_tensor(f"stick_po{h}{j}", [P, HALF], F32)) for j in range(NH)] for h in range(2)]
        block = cx.enter_context(nc.Block())

        @block.gpsimd
        def _(pool):
            co.clear_stale(pool)
            pool.sem_inc(carry_ready, C)
            with pool.Fori(0, SB_HEADS // 2) as pr:
                wait_alone(co, pool, pv_done, N * pr + S)
                pool.tensor_copy(kp[:, :], feat[:, ds(F_KS + pr, 1), :].rearrange("p o t -> p (o t)")).then_inc(kv_ready, 1)
                pool.tensor_copy(vp[:, :, :], tok[:, T_VS, :, ds(pr * P, P)]).then_inc(kv_ready, 1)

                def strict(ap, c0, done):
                    pool.affine_select(out=ap[:, c0:c0 + P], in_=ap[:, c0:c0 + P], compare_op=ALU.is_gt, fill=0.0,
                                       base=0, pattern=[[1, P]], channel_multiplier=-1).then_inc(done, 1)

                for m in range(N + 2):
                    if m < N:
                        h, th, j, c0 = work[m]
                        s = m % S
                        wait_alone(co, pool, sp_ready, N * pr + (m + 1 + S))
                        if diag[m]:
                            strict(sps[:, s, :], c0, sp_masked)
                        if carries[m]:
                            k = QB * th + QB - 1 - j
                            new, old = carry[:, h, k % 2, :], carry[:, h, (k + 1) % 2, :]
                            wait_alone(co, pool, r_full, N * pr + (m - 2 + 1 + S))
                            if diag[m]:
                                wait_alone(co, pool, sp_masked, sum(diag) * pr + (upto(diag, m)))
                            c1 = c0 + P if diag[m] else c0
                            if c1 < HALF:
                                pool.wait_ge(carry_ready, sum(adds) * pr + (upto(adds, m - 2) + C))
                                ins = pool.tensor_tensor(new[:, c1:], old[:, c1:], sps[:, s, c1:], ALU.add)
                                ins.then_inc(carry_ready, 1)
                            if diag[m]:
                                pool.tensor_copy(new[:, c0:c1], sps[:, s, c0:c1]).then_inc(carry_ready, 1)
                    if m >= 2 and diag[m - 2]:
                        wait_alone(co, pool, a_ready, N * pr + (m - 2 + 1 + S))
                        strict(aw[:, (m - 2) % S, :], work[m - 2][3], a_masked)

        @block.scalar
        def _(act):
            link = Chain(act, act_done)
            act.preload_act_table_set(LN_EXP)
            act.sem_inc(a_ready, S)
            with act.Fori(0, SB_HEADS // 2) as pr:
                act.wait_ge(pv_done, N * pr + S)
                nc.scalar.activation(qp[:, :], feat[:, ds(F_QS + pr, 1), :].rearrange("p o t -> p (o t)"), ACT.Copy,
                                     scale=SB_DH ** -0.5).then_inc(q_ready, 1)
                link.restart()
                for m in range(N + 2):
                    if m < N:
                        c0, s = work[m][3], m % S
                        act.wait_ge(z_full, N * pr + (m + 1))
                        act.wait_ge(sp_ready, N * pr + (m - S + 1 + S))
                        link(nc.scalar.activation(t[:, s, c0:], pz[s][:, c0:], ACT.Abs))
                        link(nc.scalar.activation(t[:, s, c0:], t[:, s, c0:], ACT.Exp, scale=-1.0))
                        nc.scalar.activation(t[:, s, c0:], t[:, s, c0:], ACT.Ln, bias=1.0).then_inc(logs, 1)
                    if m >= 2:
                        n = m - 2
                        c0, s = work[n][3], n % S
                        act.wait_ge(pv_done, N * pr + (n - S + 1 + S))
                        act.wait_ge(r_full, N * pr + (n + 1 + S))
                        nc.scalar.activation(aw[:, s, c0:], pz[s][:, c0:], ACT.Exp).then_inc(a_ready, 1)

        @block.vector
        def _(dve):
            dve.sem_inc(sp_ready, S)
            dve.sem_inc(o_free, 2 * NH)
            with dve.Fori(0, SB_HEADS // 2) as pr:
                for m in range(N + 5):
                    if m < N:
                        c0, s = work[m][3], m % S
                        dve.wait_ge(r_full, N * pr + (m - S + 1 + S))
                        dve.wait_ge(carry_ready, sum(adds) * pr + (upto(adds, m - S) + C))
                        dve.wait_ge(logs, N * pr + (m + 1))
                        nc.vector.scalar_tensor_tensor(sps[:, s, c0:], pz[s][:, c0:], 0.0, t[:, s, c0:],
                                                       ALU.max, ALU.add).then_inc(sp_ready, 1)
                    n = m - 4
                    if 0 <= n < N and last_of[n]:
                        h, th, _, _ = work[n]
                        rows = slice(h * SB_DH, (h + 1) * SB_DH)
                        dve.wait_ge(pv_done, N * pr + (n + 1 + S))
                        nc.vector.tensor_copy(
                            mix_t[rows, ds(GLA_HEADS + pr, 1), th * HALF:(th + 1) * HALF].rearrange("p o t -> p (o t)"),
                            po[h][th][rows, :]).then_inc(o_free, 1)

        @block.tensor
        def _(pe):
            pe.sem_inc(r_full, S)
            pe.sem_inc(pv_done, S)
            with pe.Fori(0, SB_HEADS // 2) as pr:
                wait_alone(co, pe, q_ready, pr + 1)
                wait_alone(co, pe, kv_ready, 2 * pr + 2)
                for m in range(N + 4):
                    if m < N:
                        h, th, j, c0 = work[m]
                        rows = slice(h * SB_DH, (h + 1) * SB_DH)
                        wait_alone(co, pe, a_ready, N * pr + (m - S + 1 + S))
                        nc.tensor.matmul(pz[m % S][:, c0:], kp[rows, j * P:(j + 1) * P],
                                         qp[rows, th * HALF + c0:(th + 1) * HALF], start=True, stop=False,
                                         skip_group_check=True).then_inc(z_full, 1)
                    n = m - 2
                    if 0 <= n < N:
                        h, th, j, c0 = work[n]
                        s = n % S
                        if diag[n]:
                            pe.wait_ge(sp_masked, sum(diag) * pr + (upto(diag, n)))
                        else:
                            pe.wait_ge(sp_ready, N * pr + (n + 1 + S))
                        k = QB * th + QB - 1 - j
                        c1 = c0 + P if diag[n] else c0
                        last = nc.tensor.matmul(pz[s][:, c0:], negtri[:, :], sps[:, s, c0:], start=False,
                                                stop=(c1 == HALF), skip_group_check=True)
                        if c1 < HALF:
                            pe.wait_ge(carry_ready, sum(adds) * pr + (upto(adds, n - 2) + C))
                            last = nc.tensor.matmul(pz[s][:, c1:], negone[:, :], carry[:, h, (k + 1) % 2, c1:],
                                                    start=False, stop=True, skip_group_check=True)
                        last.then_inc(r_full, 1)
                    n = m - 4
                    if 0 <= n < N:
                        h, th, j, c0 = work[n]
                        rows = slice(h * SB_DH, (h + 1) * SB_DH)
                        first = j == QB * th + QB - 1
                        if first:
                            wait_alone(co, pe, o_free, 2 * NH * pr + (2 * th + h + 1))
                        if diag[n]:
                            pe.wait_ge(a_masked, sum(diag) * pr + (upto(diag, n)))
                        else:
                            pe.wait_ge(a_ready, N * pr + (n + 1 + S))
                        nc.tensor.matmul(po[h][th][rows, c0:], vp[:, j, rows], aw[:, n % S, c0:], start=first,
                                         stop=(j == 0), skip_group_check=True).then_inc(pv_done, 1)
    co.end_phase()


def memory_attention_phase(co, q_t, k_t, v, out_t):
    nc = co.nc
    sem = lambda n: co.sem(f"mem_{n}")
    q_ready, s_full, max_ready, probs, normed, turned, turned_sb, o_full, o_taken = (
        sem(n) for n in ("q_ready", "s_full", "max_ready", "probs", "normed", "turned", "turned_sb", "o_full", "o_taken"))
    done = sem("done")
    scale = MEM_DH ** -0.5
    HD = MEM_DH // P
    with ExitStack() as cx:
        qb = co.sb("mem_qb", [P, 2, KT, P], ctx=cx)
        pr = co.sb("mem_probs", [P, 2, MEM_HEADS, MEM], ctx=cx)
        prt = co.sb("mem_probs_t", [P, MEM_HEADS * MB, P], ctx=cx)
        stat = co.sb("mem_stat", [P, 2, 4, MEM_HEADS], ctx=cx)
        ps = [cx.enter_context(nc.psum_tensor(f"mem_ps{j}", [P, MEM_HEADS, MEM], F32)) for j in range(2)]
        pt = cx.enter_context(nc.psum_tensor("mem_pt", [P, MEM_HEADS * MB, P], F32))
        po = cx.enter_context(nc.psum_tensor("mem_po", [P, KT, P], F32))
        block = cx.enter_context(nc.Block())

        @block.gpsimd
        def _(pool):
            co.clear_stale(pool)

        @block.scalar
        def _(act):
            def first(b, s):
                nc.scalar.activation(qb[:, s, :, :], q_t[:, :, ds(b * P, P)], ACT.Copy).then_inc(q_ready, 1)

            def second(b, s):
                act.wait_ge(max_ready, b + 1)
                for h in range(MEM_HEADS):
                    nc.scalar.activation(pr[:, s, h, :], ps[s][:, h, :], ACT.Exp, bias=stat[:, s, 1, h:h + 1],
                                         scale=scale, accum_out=stat[:, s, 2, h:h + 1]).then_inc(probs, 1)
                act.wait_ge(turned, b + 1)
                nc.scalar.activation(prt[:, :, :], pt[:, :, :], ACT.Copy).then_inc(turned_sb, 1)

            steps(act, first, second)

        @block.tensor
        def _(pe):
            def first(b, s):
                pe.wait_ge(q_ready, b + 1)
                for h in range(MEM_HEADS):
                    for k in range(HD):
                        last = nc.tensor.matmul(ps[s][:, h, :], qb[:, s, HD * h + k, :], k_t[:, HD * h + k, :],
                                                start=(k == 0), stop=(k == HD - 1))
                last.then_inc(s_full, 1)

            def second(b, s):
                pe.wait_ge(normed, b + 1)
                for h in range(MEM_HEADS):
                    for m in range(MB):
                        last = nc.tensor.transpose(pt[:, MB * h + m, :], pr[:, s, h, m * P:(m + 1) * P], co.ident[:, :])
                last.then_inc(turned, 1)
                pe.wait_ge(turned_sb, b + 1)
                pe.wait_ge(o_taken, b + 1)
                for h in range(MEM_HEADS):
                    for k in range(HD):
                        f = HD * h + k
                        for m in range(MB):
                            last = nc.tensor.matmul(po[:, f, :], v[:, m, f * P:(f + 1) * P], prt[:, MB * h + m, :],
                                                    start=(m == 0), stop=(m == MB - 1))
                last.then_inc(o_full, 1)

            steps(pe, first, second)

        @block.vector
        def _(dve):
            link = Chain(dve, done)
            dve.sem_inc(o_taken, 1)

            def first(b, s):
                pass

            def second(b, s):
                link.restart()
                mx, neg, tot, inv = (stat[:, s, j, :] for j in range(4))
                dve.wait_ge(s_full, b + 1)
                link(nc.vector.tensor_reduce(mx, ps[s][:, :, :], AX, ALU.max))
                nc.vector.tensor_scalar(neg, mx, -scale, None, ALU.mult).then_inc(max_ready, 1)
                dve.wait_ge(probs, MEM_HEADS * (b + 1))
                link(nc.vector.reciprocal(inv, tot))
                nc.vector.tensor_tensor(pr[:, s, :, :], pr[:, s, :, :],
                                        inv.unsqueeze(2).broadcast_to([P, MEM_HEADS, MEM]), ALU.mult).then_inc(normed, 1)
                dve.wait_ge(o_full, b + 1)
                nc.vector.tensor_copy(out_t[:, :, ds(b * P, P)], po[:, :, :]).then_inc(o_taken, 1)

            steps(dve, first, second)
    co.end_phase()


def key_scores_phase(co, act_t, weights, sub_keys, scores):
    nc = co.nc
    sem = lambda n: co.sem(f"keys_{n}")
    U = 4
    NT = 2 * PH
    landed = [sem(f"landed{j}") for j in range(U)]
    keys_landed, q_full, q_sb, s_full, s_taken = (sem(n) for n in ("keys_landed", "q_full", "q_sb", "s_full", "s_taken"))
    S = 2
    with ExitStack() as cx:
        w = [co.sb(f"keys_w{j}", [P, KT, P], ctx=cx) for j in range(U)]
        sk = co.sb("keys_sk", [P, NT, P], ctx=cx)
        qt = co.sb("keys_qt", [P, S, SEQ], ctx=cx)
        pq = [cx.enter_context(nc.psum_tensor(f"keys_pq{j}", [P, SEQ], F32)) for j in range(S)]
        pss = [cx.enter_context(nc.psum_tensor(f"keys_ps{j}", [P, NB, P], F32)) for j in range(S)]
        block = cx.enter_context(nc.Block())

        @block.gpsimd
        def _(pool):
            co.clear_stale(pool)

        @block.sync
        def _(sp):
            for j in range(U):
                sp.dma_start(w[j][:, :, :].rearrange("p k c -> p (k c)"), weights[j]).then_inc(landed[j], 16)
                if j == 0:
                    sp.dma_start(sk[:, :, :], sub_keys).then_inc(keys_landed, 16)
            with sp.Fori(0, NT // U - 1) as i:
                for j in range(U):
                    sp.wait_ge(q_full, U * i + j + 1)
                    sp.dma_start(w[j][:, :, :].rearrange("p k c -> p (k c)"),
                                 weights[ds(U * i + U + j, 1)].rearrange("o p c -> p (o c)")).then_inc(landed[j], 16)

        @block.tensor
        def _(pe):
            pe.sem_inc(s_full, S)

            def products(n, j):
                pe.wait_ge(q_sb, n + 1 + S)
                pe.wait_ge(s_taken, n + 1)
                for b in range(NB):
                    last = nc.tensor.matmul(pss[j % S][:, b, :], qt[:, j % S, b * P:(b + 1) * P],
                                            sk[:, ds(n, 1), :].rearrange("p o c -> p (o c)"), start=True, stop=True)
                last.then_inc(s_full, 1)

            pe.wait_ge(keys_landed, 16)
            with pe.Fori(0, NT // U) as i:
                for j in range(U):
                    pe.wait_ge(landed[j], 16 * i + 16)
                    pe.wait_ge(q_sb, U * i + j + 1)
                    for h in range(SEQ // HALF):
                        cols = slice(h * HALF, (h + 1) * HALF)
                        for k in range(KT):
                            last = nc.tensor.matmul(pq[j % S][:, cols], w[j][:, k, :], act_t[:, k, cols],
                                                    start=(k == 0), stop=(k == KT - 1))
                    last.then_inc(q_full, 1)
                    if j:
                        products(U * i + j - 1, j - 1)
                products(U * i + U - 1, U - 1)

        @block.scalar
        def _(act):
            act.sem_inc(q_sb, S)
            with act.Fori(0, NT // U) as i:
                for j in range(U):
                    act.wait_ge(q_full, U * i + j + 1)
                    act.wait_ge(s_full, U * i + j + 1)
                    nc.scalar.activation(qt[:, j % S, :], pq[j % S][:, :], ACT.Copy).then_inc(q_sb, 1)

        @block.vector
        def _(dve):
            dve.sem_inc(s_taken, S)
            with dve.Fori(0, NT // U) as i:
                for j in range(U):
                    dve.wait_ge(s_full, U * i + j + 1 + S)
                    nc.vector.tensor_copy(scores[:, :, ds(U * i + j, 1), :].rearrange("p b o c -> p (b o) c"),
                                          pss[j % S][:, :, :]).then_inc(s_taken, 1)
    co.end_phase()


def expert_phase(co, scores, rstd, uv, g_ffn, g_final, out):
    nc = co.nc
    sem = lambda n: co.sem(f"expert_{n}")
    G = NB * PH
    ROWS = PB = 8
    DG = 4
    E = 2 * D
    landed = [sem(f"landed{j}") for j in range(ROWS)]
    (gains_landed, iota_ready, s_ready, best_ready, exp_ready, index_ready, gate_ready, dots, diag_ready, row_used,
     acc_taken, var_ready, guess_ready, out_ready, stored, done, act_done, dot_done) = (
        sem(n) for n in ("gains_landed", "iota_ready", "s_ready", "best_ready", "exp_ready", "index_ready", "gate_ready",
                         "dots", "diag_ready", "row_used", "acc_taken", "var_ready", "guess_ready", "out_ready",
                         "stored", "done", "act_done", "dot_done"))
    with ExitStack() as cx:
        sb = lambda n, shape, dt=F32: co.sb(f"expert_{n}", shape, dt, ctx=cx)
        more = sb("rows", [P, ROWS - KT // 2, E])
        rows = [co.XT[:, 2 * j:2 * j + 2, :].rearrange("p a d -> p (a d)") for j in range(KT // 2)]
        rows += [more[:, j, :] for j in range(ROWS - KT // 2)]
        gf, gl = sb("gffn", [P, D]), sb("gfinal", [P, D])
        xn, hb, ob = sb("xn", [P, D]), sb("hb", [P, D]), sb("ob", [P, D])
        s_in = sb("s_in", [P, 2, 2, NKEYS])
        s_rest = sb("s_rest", [P, NKEYS])
        top = sb("top", [P, 2, TOPK])
        top_i = sb("top_i", [P, 2, TOPK], U32)
        top_f = sb("top_f", [P, 2, TOPK])
        cand = sb("cand", [P, TOPK, TOPK])
        cand_rest = sb("cand_rest", [P, TOPK, TOPK])
        best = sb("best", [P, 2, TOPK])
        best_j = sb("best_j", [P, TOPK], U32)
        pos = sb("pos", [P, 2, TOPK], U32)
        pos_f = sb("pos_f", [P, 2, TOPK])
        iota = sb("iota", [P, TOPK])
        hot = sb("hot", [P, 2, TOPK, TOPK])
        picked = sb("picked", [P, 2, TOPK])
        index = sb("index", [P, 2, TOPK], U32)
        gate = sb("gate", [P, 2, TOPK])
        small = sb("small", [P, 6])
        small2 = sb("small2", [P, 4])
        dot = sb("dot", [P, 2, TOPK])
        wt = sb("wt", [P, 2, 2, TOPK])
        dg = sb("dg", [P, DG, P])
        acc = cx.enter_context(nc.psum_tensor("expert_acc", [P, D], F32))
        junk = cx.enter_context(nc.psum_tensor("expert_junk", [P, D], F32))
        block = cx.enter_context(nc.Block())
        groups = scores.rearrange("p b (h c) n -> p (b h) (c n)", c=2)

        def over_groups(eng, group, before=None, after=None):
            with eng.Fori(0, NB) as b:
                if before:
                    before(b)
                with eng.Fori(0, PH // 2) as i:
                    for s in range(2):
                        group(PH * b + 2 * i + s, s)
                if after:
                    after(b)

        @block.sync
        def _(sp):
            sp.dma_start(gf[:, :], g_ffn.broadcast_to([P, D])).then_inc(gains_landed, 16)
            sp.dma_start(gl[:, :], g_final.broadcast_to([P, D])).then_inc(gains_landed, 16)
            sp.sem_inc(stored, 16)
            with sp.Fori(0, NB) as b:
                wait_alone(co, sp, out_ready, b + 1)
                sp.dma_start(out[ds(b, 1)].rearrange("o p d -> p (o d)"), ob[:, :]).then_inc(stored, 16)
                wait_alone(co, sp, stored, 16 * b + 32)

        @block.gpsimd
        def _(pool):
            co.clear_stale(pool)
            pool.iota(iota[:, :], pattern=[[1, TOPK]], base=0, channel_multiplier=0,
                      allow_small_or_imprecise_dtypes=True).then_inc(iota_ready, 1)

            def group(g, s):
                wait_alone(co, pool, index_ready, g + 1)
                for r in range(TOPK):
                    wait_alone(co, pool, row_used, TOPK * g + r + 1)
                    pool.indirect_dma_start(
                        out=rows[r % ROWS], out_offset=None, in_=uv,
                        in_offset=bass.IndirectOffsetOnAxis(ap=index[:, s, r:r + 1], axis=0),
                        bounds_check=NKEYS * NKEYS - 1, oob_is_err=False).then_inc(landed[r % ROWS], 16)

            over_groups(pool, group)

        @block.vector
        def _(dve):
            link = Chain(dve, done)
            LOWEST = -3.0e38

            def top16(value, index_out, values, rest, flat=lambda x: x):
                for e in range(2):
                    part = slice(8 * e, 8 * e + 8)
                    src = values if e == 0 else rest
                    link(nc.vector.max(value[:, part], src))
                    link(nc.vector.max_index(index_out[:, part], value[:, part], src))
                    if e == 0:
                        link(nc.vector.match_replace(rest, value[:, part], src, LOWEST))

            def select(g, s):
                link.restart()
                wait_alone(co, dve, s_ready, g + 1)
                for c in range(2):
                    top16(top[:, c, :], top_i[:, c, :], s_in[:, s, c, :], s_rest[:, :])
                link(nc.vector.tensor_copy(top_f[:, :, :], top_i[:, :, :]))
                link(nc.vector.tensor_tensor(cand[:, :, :], top[:, 0, :].unsqueeze(2).broadcast_to([P, TOPK, TOPK]),
                                             top[:, 1, :].unsqueeze(1).broadcast_to([P, TOPK, TOPK]), ALU.add))
                flat = lambda x: x[:, :, :].rearrange("p a b -> p (a b)")
                top16(best[:, s, :], best_j[:, :], flat(cand), flat(cand_rest))
                link(nc.vector.tensor_scalar(small[:, s:s + 1], best[:, s, 0:1], -1.0, None, ALU.mult))
                dve.sem_inc(best_ready, 1)
                link(nc.vector.tensor_scalar(pos[:, 0, :], best_j[:, :], 4, None, ALU.logical_shift_right))
                link(nc.vector.tensor_scalar(pos[:, 1, :], best_j[:, :], TOPK - 1, None, ALU.bitwise_and))
                link(nc.vector.tensor_copy(pos_f[:, :, :], pos[:, :, :]))
                for c in range(2):
                    link(nc.vector.tensor_tensor(hot[:, c, :, :], pos_f[:, c, :].unsqueeze(2).broadcast_to([P, TOPK, TOPK]),
                                                 iota[:, :].unsqueeze(1).broadcast_to([P, TOPK, TOPK]), ALU.is_equal))
                    link(nc.vector.tensor_tensor(hot[:, c, :, :], hot[:, c, :, :],
                                                 top_f[:, c, :].unsqueeze(1).broadcast_to([P, TOPK, TOPK]), ALU.mult))
                link(nc.vector.tensor_reduce(picked[:, :, :], hot[:, :, :, :], AX, ALU.add))
                link(nc.vector.scalar_tensor_tensor(index[:, s, :], picked[:, 0, :], float(NKEYS), picked[:, 1, :],
                                                    ALU.mult, ALU.add))
                dve.sem_inc(index_ready, 1)
                dve.wait_ge(exp_ready, g + 1)
                link(nc.vector.reciprocal(small[:, 4 + s:5 + s], small[:, 2 + s:3 + s]))
                link(nc.vector.tensor_scalar(gate[:, s, :], best[:, s, :], small[:, 4 + s:5 + s], None, ALU.mult))
                dve.sem_inc(gate_ready, 1)

            def group(g, s):
                select(g + 1, 1 - s)
                for r in range(TOPK):
                    dve.wait_ge(landed[r % ROWS], 16 * (TOPK // ROWS * g + r // ROWS + 1))
                    link(nc.vector.tensor_tensor_reduce(junk[:, :], rows[r % ROWS][:, 0:D], xn[:, :], 1.0, 0.0,
                                                        ALU.mult, ALU.add, dot[:, s, r:r + 1]))
                    dve.sem_inc(dots, 1)

            def before(b):
                link.restart()
                link(nc.vector.scalar_tensor_tensor(xn[:, :], co.H[:, ds(b, 1), :].rearrange("p o d -> p (o d)"),
                                                    rstd[:, ds(b, 1)], gf[:, :], ALU.mult, ALU.mult))

            def after(b):
                link.restart()
                dve.wait_ge(row_used, TOPK * PH * (b + 1) + ROWS)
                link(nc.vector.tensor_copy(hb[:, :], acc[:, :]))
                dve.sem_inc(acc_taken, 1)
                ms, var, tmp, y = (small2[:, j:j + 1] for j in range(4))
                link(nc.vector.tensor_tensor_reduce(junk[:, :], hb[:, :], hb[:, :], 1.0, 0.0, ALU.mult, ALU.add, ms))
                nc.vector.tensor_scalar(var, ms, 1.0 / D, EPS, ALU.mult, ALU.add).then_inc(var_ready, 1)
                dve.wait_ge(guess_ready, b + 1)
                rstd_steps(link, nc, ms, var, tmp, y)
                dve.wait_ge(stored, 16 * b + 16)
                nc.vector.scalar_tensor_tensor(ob[:, :], hb[:, :], y, gl[:, :], ALU.mult, ALU.mult).then_inc(out_ready, 1)

            dve.sem_inc(acc_taken, 1)
            dve.wait_ge(iota_ready, 1)
            dve.wait_ge(gains_landed, 32)
            select(0, 0)
            over_groups(dve, group, before, after)

        @block.scalar
        def _(act):
            link = Chain(act, act_done)

            def scores_in(g, s):
                nc.scalar.activation(s_in[:, s, :, :].rearrange("p c n -> p (c n)"),
                                     groups[:, ds(g % G, 1), :].rearrange("p o n -> p (o n)"), ACT.Copy).then_inc(s_ready, 1)

            def exps(g, s):
                act.wait_ge(best_ready, g + 1)
                link(nc.scalar.activation(best[:, s, :], best[:, s, :], ACT.Exp, bias=small[:, s:s + 1],
                                          accum_out=small[:, 2 + s:3 + s]))
                act.sem_inc(exp_ready, 1)

            def group(g, s):
                link.restart()
                act.wait_ge(index_ready, g + 1)
                scores_in(g + 2, s)
                exps(g + 1, 1 - s)
                act.wait_ge(gate_ready, g + 1)
                for r in range(TOPK):
                    act.wait_ge(dots, TOPK * g + r + 1)
                    link(nc.scalar.activation(wt[:, s, 0, r:r + 1], dot[:, s, r:r + 1], ACT.Gelu))
                    link(nc.scalar.activation(wt[:, s, 1, r:r + 1], wt[:, s, 0, r:r + 1], ACT.Copy,
                                              scale=gate[:, s, r:r + 1]))
                    act.wait_ge(row_used, TOPK * g + r + 1 + ROWS - DG)
                    nc.scalar.activation(dg[:, r % DG, :], co.ident[:, :], ACT.Copy,
                                         scale=wt[:, s, 1, r:r + 1]).then_inc(diag_ready, 1)

            def after(b):
                act.preload_act_table_set(LN_EXP)
                link.restart()
                act.wait_ge(var_ready, b + 1)
                link(nc.scalar.activation(small2[:, 2:3], small2[:, 1:2], ACT.Ln))
                nc.scalar.activation(small2[:, 3:4], small2[:, 2:3], ACT.Exp, scale=-0.5).then_inc(guess_ready, 1)

            scores_in(0, 0)
            scores_in(1, 1)
            exps(0, 0)
            over_groups(act, group, None, after)

        @block.tensor
        def _(pe):
            pe.sem_inc(row_used, ROWS)

            def before(b):
                pe.wait_ge(acc_taken, b + 1)
                for h in range(2):
                    nc.tensor.matmul(acc[:, h * HALF:(h + 1) * HALF], co.ident[:, :],
                                     co.H[:, ds(b, 1), h * HALF:(h + 1) * HALF].rearrange("p o d -> p (o d)"),
                                     start=True, stop=False, skip_group_check=True)

            def group(g, s):
                for r in range(TOPK):
                    pe.wait_ge(diag_ready, TOPK * g + r + 1)
                    for h in range(2):
                        last = nc.tensor.matmul(acc[:, h * HALF:(h + 1) * HALF], dg[:, r % DG, :],
                                                rows[r % ROWS][:, D + h * HALF:D + (h + 1) * HALF],
                                                start=False, stop=False, skip_group_check=True)
                    last.then_inc(row_used, 1)

            over_groups(pe, group, before)
    co.end_phase()


def program(nc, a, out):
    with ExitStack() as ctx:
        co = Core(nc, ctx)
        co.steps = ctx.enter_context(nc.semaphore("steps"))
        co.ident = co.sb("ident", [P, P])
        co.H = co.sb("H", [P, NB, D])
        co.XT = co.sb("XT", [P, KT, SEQ])
        gains = co.sb("gains", [P, 4, KT])
        negtri, negone = co.sb("negtri", [P, P]), co.sb("negone", [P, P])
        rstd = co.sb("rstd", [P, NB])
        prep = ctx.enter_context(nc.semaphore("prep"))
        gl = ctx.enter_context(nc.semaphore("gl"))
        with nc.Block() as block:
            @block.gpsimd
            def _(pool):
                pool.memset(co.ident[:, :], 0.0).then_inc(prep, 1)
                pool.memset(negone[:, :], -1.0).then_inc(prep, 1)
                pool.memset(negtri[:, :], -1.0).then_inc(prep, 1)
                pool.wait_ge(prep, 3)
                pool.affine_select(out=negtri[:, :], in_=negtri[:, :], compare_op=ALU.is_ge, fill=0.0,
                                   base=0, pattern=[[-1, P]], channel_multiplier=1).then_inc(prep, 1)
                pool.affine_select(out=co.ident[:, :], in_=co.ident[:, :], compare_op=ALU.not_equal, fill=1.0,
                                   base=0, pattern=[[-1, P]], channel_multiplier=1).then_inc(prep, 1)
            @block.sync
            def _(sp):
                sp.dma_start(gains[:, :, :], a['gains'][:, :, :]).then_inc(gl, 16)
                sp.wait_ge(gl, 16)
        xv = a['x'].rearrange("(b p) d -> p b d", p=P)
        norm_phase(co, "mixnorm", co.H, NB, gains[:, 0, :], co.XT, rstd[:, :],
                   loads=[(co.H[:, 2 * j:2 * j + 2, :], xv[:, 2 * j:2 * j + 2, :]) for j in range(4)])
        with ExitStack() as mix:
            feat = co.sb("feat", [P, NFEAT, SEQ], ctx=mix)
            tok = co.sb("tok", [P, NTOK, NB, HALF], ctx=mix)
            feature_gemm_phase(co, "mixfeat", co.XT, SEQ, a['w_feat'], NFEAT, feat)
            token_gemm_phase(co, "mixtok", co.XT, NB, a['w_tok'], NTOK,
                             lambda c, b, bank: nc.vector.tensor_copy(tok[:, ds(c, 1), b, :].rearrange("p o c -> p (o c)"), bank[:, :]))
            with ExitStack() as gl:
                decay = co.sb("decay", [P, 2, SEQ], ctx=gl)
                decay_phase(co, co.XT, a['w_alr'], a['w_up'], a['b_alpha'], decay)
                gla_phase(co, feat, tok, decay)
            gla_norm_phase(co, tok, a['g_gla'], co.XT)
            stick_phase(co, feat, tok, co.XT, negtri, negone)
            def add(c, b, bank):
                h = co.H[:, b, ds(c * HALF, HALF)]
                return nc.vector.tensor_tensor(h, h, bank[:, :], ALU.add)
            token_gemm_phase(co, "mixout", co.XT, NB, a['w_out'], D // HALF, add)
        with ExitStack() as mem:
            q_t = co.sb("q_t", [P, KT, SEQ], ctx=mem)
            k_t = co.sb("k_t", [P, KT, MEM], ctx=mem)
            v_m = co.sb("v_m", [P, MB, D], ctx=mem)
            m_tok = co.sb("m_tok", [P, MB, D], ctx=mem)
            m_t = co.sb("m_t", [P, KT, MEM], ctx=mem)
            norm_phase(co, "memnorm", m_tok, MB, gains[:, 2, :], m_t, rstd[:, 0:MB],
                       loads=[(m_tok[:, :, :], a['mem'].rearrange("(b p) d -> p b d", p=P))])
            feature_gemm_phase(co, "memk", m_t, MEM, a['w_mk'], KT, k_t)
            token_gemm_phase(co, "memv", m_t, MB, a['w_mv'], D // HALF,
                             lambda c, b, bank: nc.vector.tensor_copy(v_m[:, b, ds(c * HALF, HALF)], bank[:, :]))
            norm_phase(co, "qnorm", co.H, NB, gains[:, 1, :], co.XT, rstd[:, :])
            feature_gemm_phase(co, "memq", co.XT, SEQ, a['w_mq'], KT, q_t)
            memory_attention_phase(co, q_t, k_t, v_m, co.XT)
        token_gemm_phase(co, "memout", co.XT, NB, a['w_mo'], D // HALF, add)
        norm_phase(co, "ffnnorm", co.H, NB, gains[:, 3, :], co.XT, rstd[:, :])
        scores = co.sb("scores", [P, NB, 2 * PH, NKEYS])
        key_scores_phase(co, co.XT, a['w_pq'], a['sub_keys'], scores)
        expert_phase(co, scores[:, :, :, :], rstd, a['uv'], a['g_ffn'], a['g_final'],
                     out.rearrange("(b p) d -> b p d", p=P))


def kernel(**inputs):
    import numpy as np
    import concourse.bacc as bacc
    from concourse.bass_utils import run_bass_kernel_spmd

    i = {k: np.asarray(v) for k, v in inputs.items()}

    def by_feature(v):
        return v.reshape(-1, P).T

    def column_tiles(w, width):
        n = w.shape[1] // width
        return w.reshape(KT, P, n, width).transpose(2, 1, 0, 3).reshape(n, P, KT * width)

    w_in = i["w_in"][0]
    bounds = np.cumsum([GLA_HEADS * GLA_DK, GLA_HEADS * GLA_DK, GLA_HEADS * GLA_DV, GLA_HEADS * GLA_DV, RANK,
                        SB_HEADS * SB_DH, SB_HEADS * SB_DH])
    qg, kg, vg, og, alr, qs, ks, vs = np.split(w_in, bounds, axis=1)
    w_mkv = i["w_mkv"][0]
    arrays = {
        "x": i["x"][0],
        "mem": i["mem"][0],
        "gains": np.stack([by_feature(i[n][0]) for n in ("g_mix", "g_mem_q", "g_mem_kv", "g_ffn")], axis=1),
        "w_feat": column_tiles(np.concatenate([qg, kg, qs, ks], axis=1), P),
        "w_tok": column_tiles(np.concatenate([vg, og, vs], axis=1), HALF),
        "w_alr": alr.reshape(KT, P, RANK).transpose(1, 0, 2),
        "w_up": i["w_alpha_up"][0],
        "b_alpha": by_feature(i["b_alpha"][0]),
        "g_gla": by_feature(i["g_gla_out"][0]),
        "w_out": column_tiles(i["w_out"][0], HALF),
        "w_mq": column_tiles(i["w_mq"][0], P),
        "w_mk": column_tiles(w_mkv[:, :D], P),
        "w_mv": column_tiles(w_mkv[:, D:], HALF),
        "w_mo": column_tiles(i["w_mo"][0], HALF),
        "w_pq": column_tiles(i["w_pq"][0], P),
        "sub_keys": i["sub_keys"][0].reshape(2 * PH, NKEYS, P).transpose(2, 0, 1),
        "uv": np.concatenate([i["peer_u"][0], i["peer_v"][0]], axis=1),
        "g_ffn": i["g_ffn"][0:1],
        "g_final": i["g_final"].reshape(1, D),
    }
    arrays = {f"in_{k}": np.ascontiguousarray(v) for k, v in arrays.items()}
    nc = bacc.Bacc("TRN2", target_bir_lowering=False, num_devices=1)
    a = {k[3:]: nc.dram_tensor(k, v.shape, mybir.dt.from_np(v.dtype), kind="ExternalInput").ap()
         for k, v in arrays.items()}
    out = nc.dram_tensor("out_0", (SEQ, D), F32, kind="ExternalOutput").ap()
    program(nc, a, out)
    r = run_bass_kernel_spmd(nc, [arrays], core_ids=[0])
    return r.results[0]["out_0"].reshape(1, SEQ, D)
```

```python
from contextlib import ExitStack

import concourse.bass as bass
from concourse import mybir

F32 = mybir.dt.float32
F32R = mybir.dt.float32r
U32 = mybir.dt.uint32
ALU = mybir.AluOpType
ACT = mybir.ActivationFunctionType
AX = mybir.AxisListType.X
ds = bass.ds

P = 128
SEQ = 1024
D = 1024
KT = D // P
NB = SEQ // P
HALF = 512
EPS = 1e-6

GLA_HEADS, GLA_DK, GLA_DV, RANK, TAU = 4, 64, 128, 16, 16.0
CHUNK = 64
SUB = 16
NSUB = CHUNK // SUB
SB_HEADS, SB_DH = 8, 64
MEM, MEM_HEADS, MEM_DH = 256, 4, 256
MB = MEM // P
PH, NKEYS, TOPK = 8, 128, 16
EXP_CAP = 80.0
LN_EXP = "natural_log_exp_and_others"

F_QG, F_KG, F_QS, F_KS, NFEAT = 0, 2, 4, 8, 12
T_VG, T_OG, T_VS, NTOK = 0, 1, 2, 3


class Chain:

    def __init__(self, eng, sem):
        self.eng, self.sem, self.n = eng, sem, 0

    def __call__(self, ins):
        self.n += 1
        ins.then_inc(self.sem, 1)
        self.eng.wait_ge(self.sem, self.n)

    def restart(self):
        self.eng.sem_clear(self.sem)
        self.n = 0


def wait_alone(co, eng, sem, value):
    eng.wait_ge(sem, value)
    eng.sem_inc(co.steps, 1)


class Core:

    def __init__(self, nc, ctx):
        self.nc, self.ctx = nc, ctx
        self.phase_sems, self.stale = [], []

    def sem(self, name):
        self.phase_sems.append(self.nc.alloc_semaphore(name=name))
        return self.phase_sems[-1]

    def end_phase(self):
        self.stale, self.phase_sems = self.phase_sems, []
        for s in self.stale:
            self.nc.release_semaphore(s)

    def clear_stale(self, pool):
        for s in self.stale:
            pool.sem_clear(s)

    def sb(self, name, shape, dt=F32, ctx=None):
        return (ctx or self.ctx).enter_context(self.nc.sbuf_tensor(name, shape, dt))


def ahead(eng, n, unroll, first, second):
    first(0, 0)
    if n > unroll:
        with eng.Fori(0, n // unroll - 1) as i:
            for j in range(unroll):
                first(unroll * i + (j + 1), (j + 1) % unroll)
                second(unroll * i + j, j)
    for j in range(unroll):
        if j + 1 < unroll:
            first(n - unroll + j + 1, j + 1)
        second(n - unroll + j, j)


def steps(eng, first, second):
    ahead(eng, NB, 2, first, second)


def high(nc, hi, x):
    return nc.scalar.activation(hi, x, ACT.Copy)


def low(nc, lo, x, hi):
    return nc.vector.tensor_tensor(lo, x, hi.bitcast(F32), ALU.subtract)


def product(nc, out, w, x, start, stop):
    (wh, wl), (xh, xl) = w, x
    nc.tensor.matmul(out, wl, xh, start=start, stop=False)
    nc.tensor.matmul(out, wh, xl, start=False, stop=False)
    return nc.tensor.matmul(out, wh, xh, start=False, stop=stop)


def rstd_steps(link, nc, ms, v, t, y):
    for _ in range(2):
        link(nc.vector.tensor_tensor(t, y, y, ALU.mult))
        link(nc.vector.tensor_tensor(t, t, v, ALU.mult))
        link(nc.vector.tensor_scalar(t, t, -0.5, 1.5, ALU.mult, ALU.add))
        link(nc.vector.tensor_tensor(y, y, t, ALU.mult))


def norm_phase(co, name, tok, nb, gain, feat, rstd, loads=()):
    nc = co.nc
    sem = lambda n: co.sem(f"{name}_{n}")
    landed = [sem(f"landed{i}") for i in range(len(loads))]
    sums_a, var_ready, guess_ready, rstd_ready = sem("sums_a"), sem("var_ready"), sem("guess_ready"), sem("rstd_ready")
    scaled, turned, gained, hi_ready, act_done, done = (sem("scaled"), sem("turned"), sem("gained"), sem("hi_ready"),
                                                        sem("act_done"), sem("done"))
    parted = sem("parted")
    per = nb // max(1, len(loads))
    S = 2
    hi, lo = feat
    with ExitStack() as cx:
        ms = co.sb(f"{name}_ms", [P, nb], ctx=cx)
        var = co.sb(f"{name}_var", [P, nb], ctx=cx)
        tmp = co.sb(f"{name}_tmp", [P, nb], ctx=cx)
        xs = co.sb(f"{name}_xs", [P, S, D], ctx=cx)
        full = co.sb(f"{name}_full", [P, S, KT, P], ctx=cx)
        pt = [cx.enter_context(nc.psum_tensor(f"{name}_pt{j}", [P, KT, P], F32)) for j in range(S)]
        junk = [cx.enter_context(nc.psum_tensor(f"{name}_junk{j}", [P, D], F32)) for j in range(2)]
        block = cx.enter_context(nc.Block())
        cols = lambda b: ds(b * P, P)

        @block.gpsimd
        def _(pool):
            co.clear_stale(pool)

        @block.sync
        def _(sp):
            for s, (dst, src) in zip(landed, loads):
                sp.dma_start(dst, src).then_inc(s, 16)

        @block.scalar
        def _(act):
            act.preload_act_table_set(LN_EXP)
            link = Chain(act, act_done)
            for b in range(0, nb, 2):
                if loads:
                    act.wait_ge(landed[b // per], 16)
                link(nc.scalar.activation(junk[0][:, :], tok[:, b, :], ACT.Square, accum_out=ms[:, b:b + 1]))
            act.sem_inc(sums_a, 1)
            act.wait_ge(var_ready, 1)
            link(nc.scalar.activation(tmp[:, :], var[:, :], ACT.Ln))
            nc.scalar.activation(rstd, tmp[:, :], ACT.Exp, scale=-0.5).then_inc(guess_ready, 1)

            def scale(b, s):
                act.wait_ge(turned, b + 1)
                nc.scalar.activation(xs[:, s, :], tok[:, ds(b, 1), :].rearrange("p o d -> p (o d)"), ACT.Copy,
                                     scale=rstd[:, ds(b, 1)]).then_inc(scaled, 1)

            def part(b, s):
                act.wait_ge(gained, b + (1 + S))
                high(nc, hi[:, :, cols(b)], full[:, s, :, :]).then_inc(hi_ready, 1)

            act.wait_ge(rstd_ready, 1)
            ahead(act, nb, 2, scale, part)

        @block.vector
        def _(dve):
            link = Chain(dve, done)
            for b in range(1, nb, 2):
                if loads:
                    dve.wait_ge(landed[b // per], 16)
                link(nc.vector.tensor_tensor_reduce(junk[1][:, :], tok[:, b, :], tok[:, b, :], 1.0, 0.0,
                                                    ALU.mult, ALU.add, ms[:, b:b + 1]))
            dve.wait_ge(sums_a, 1)
            nc.vector.tensor_scalar(var[:, :], ms[:, :], 1.0 / D, EPS, ALU.mult, ALU.add).then_inc(var_ready, 1)
            dve.wait_ge(guess_ready, 1)
            rstd_steps(link, nc, ms[:, :], var[:, :], tmp[:, :], rstd)
            dve.sem_inc(rstd_ready, 1)
            dve.sem_inc(gained, S)
            dve.sem_inc(parted, S)

            def take(b, s):
                dve.wait_ge(turned, b + (1 + S))
                dve.wait_ge(parted, b + 1)
                nc.vector.tensor_tensor(full[:, s, :, :], pt[s][:, :, :], gain.unsqueeze(2).broadcast_to([P, KT, P]),
                                        ALU.mult).then_inc(gained, 1)

            def part(b, s):
                dve.wait_ge(hi_ready, b + 1)
                low(nc, lo[:, :, cols(b)], full[:, s, :, :], hi[:, :, cols(b)]).then_inc(parted, 1)

            ahead(dve, nb, 2, take, part)

        @block.tensor
        def _(pe):
            pe.sem_inc(turned, S)
            with pe.Fori(0, nb // 2) as i:
                for s in range(S):
                    pe.wait_ge(scaled, 2 * i + s + 1)
                    pe.wait_ge(gained, 2 * i + s + 1)
                    for k in range(KT):
                        last = nc.tensor.transpose(pt[s][:, k, :], xs[:, s, k * P:(k + 1) * P], co.ident[:, :])
                    last.then_inc(turned, 1)
    co.end_phase()


class Weights:

    def __init__(self, co, name, ctx, per, used, raw_slots=4, U=4):
        nc, self.co, self.per, self.used, self.R, self.U = co.nc, co, per, used, raw_slots, U
        self.landed = [co.sem(f"{name}_landed{j}") for j in range(raw_slots)]
        self.hi_ready, self.ready = co.sem(f"{name}_hi_ready"), co.sem(f"{name}_ready")
        self.raw = co.sb(f"{name}_raw", [P, raw_slots, KT * P], ctx=ctx)
        self.hi = co.sb(f"{name}_hi", [P, 2, KT * P], F32R, ctx=ctx)
        self.lo = co.sb(f"{name}_lo", [P, 2, KT * P], F32R, ctx=ctx)

    def loads(self, sp, n, piece, first=None):
        U, R = self.U, self.R

        def load(m, r):
            sp.dma_start(self.raw[:, r, :], piece(m)).then_inc(self.landed[r], 16)

        for m in range(R):
            load(m, m)
        if first:
            first()
        if n > U:
            with sp.Fori(0, n // U - 1) as i:
                for j in range(U):
                    sp.wait_ge(self.ready, U * i + (j + 1))
                    load(U * i + (j + R), j % R)
        for j in range(U - R):
            sp.wait_ge(self.ready, n - U + j + 1)
            load(n - U + j + R, j % R)

    def highs(self, act, n, j):
        act.wait_ge(self.landed[j % self.R], self.turn(n, j))
        act.wait_ge(self.used, self.per * (n + 1))
        high(self.co.nc, self.hi[:, j % 2, :], self.raw[:, j % self.R, :]).then_inc(self.hi_ready, 1)

    def turn(self, n, j):
        return (n - j) * (16 // self.R) + 16 * (j // self.R + 1)

    def lows(self, dve, n, j):
        dve.wait_ge(self.hi_ready, n + 1)
        low(self.co.nc, self.lo[:, j % 2, :], self.raw[:, j % self.R, :], self.hi[:, j % 2, :]).then_inc(self.ready, 1)

    def operand(self, j, cols):
        return self.hi[:, j % 2, cols], self.lo[:, j % 2, cols]


def feature_gemm_phase(co, name, act_t, width, weights, n_tiles, out):
    nc = co.nc
    step = min(width, HALF)
    parts = width // step
    bank_full, bank_free = co.sem(f"{name}_bank_full"), co.sem(f"{name}_bank_free")
    xh, xl = act_t
    with ExitStack() as cx:
        w = Weights(co, name, cx, parts, bank_full)
        U = w.U
        banks = [cx.enter_context(nc.psum_tensor(f"{name}_bank{j}", [P, HALF], F32)) for j in range(U * parts)]
        block = cx.enter_context(nc.Block())

        @block.gpsimd
        def _(pool):
            co.clear_stale(pool)

        @block.sync
        def _(sp):
            w.loads(sp, n_tiles, lambda m: weights[ds(m, 1)].rearrange("o p c -> p (o c)"))

        @block.tensor
        def _(pe):
            pe.sem_inc(bank_full, 2 * parts)
            with pe.Fori(0, n_tiles // U) as i:
                for j in range(U):
                    pe.wait_ge(w.ready, U * i + (j + 1))
                    for h in range(parts):
                        cols = slice(h * step, (h + 1) * step)
                        pe.wait_ge(bank_free, U * parts * i + (parts * j + h + 1))
                        for k in range(KT):
                            last = product(nc, banks[parts * j + h][:, 0:step], w.operand(j, slice(k * P, (k + 1) * P)),
                                           (xh[:, k, cols], xl[:, k, cols]), k == 0, k == KT - 1)
                        last.then_inc(bank_full, 1)

        @block.scalar
        def _(act):
            with act.Fori(0, n_tiles // U) as i:
                for j in range(U):
                    w.highs(act, U * i + j, j)

        @block.vector
        def _(dve):
            dve.sem_inc(bank_free, U * parts)

            def empty(n, j):
                for h in range(parts):
                    dve.wait_ge(bank_full, parts * n + (2 * parts + h + 1))
                    nc.vector.tensor_copy(out[:, ds(n, 1), h * step:(h + 1) * step].rearrange("p o t -> p (o t)"),
                                          banks[parts * j + h][:, 0:step]).then_inc(bank_free, 1)

            ahead(dve, n_tiles, U, lambda n, j: w.lows(dve, n, j), empty)
    co.end_phase()


def token_gemm_phase(co, name, act_t, nb, weights, n_chunks, evac, loads=()):
    nc = co.nc
    piece_done, bank_free = co.sem(f"{name}_piece_done"), co.sem(f"{name}_bank_free")
    extra = co.sem(f"{name}_extra")
    xh, xl = act_t
    KP = KT * P // HALF
    with ExitStack() as cx:
        w = Weights(co, name, cx, nb, piece_done)
        U = w.U
        banks = [cx.enter_context(nc.psum_tensor(f"{name}_bank{j}", [P, HALF], F32)) for j in range(nb)]
        block = cx.enter_context(nc.Block())

        @block.gpsimd
        def _(pool):
            co.clear_stale(pool)

        @block.sync
        def _(sp):
            def more():
                for dst, src in loads:
                    sp.dma_start(dst, src).then_inc(extra, 16)
            w.loads(sp, U * n_chunks, lambda m: weights[ds(m, 1)].rearrange("o p c -> p (o c)"), more)

        @block.tensor
        def _(pe):
            pe.sem_inc(piece_done, 2 * nb)
            with pe.Fori(0, n_chunks) as c:
                for j in range(U):
                    pe.wait_ge(w.ready, U * c + (j + 1))
                    for b in range(nb):
                        if j == 0:
                            pe.wait_ge(bank_free, nb * c + (b + 1))
                        for q in range(KP):
                            k = KP * j + q
                            tokens = slice(b * P, (b + 1) * P)
                            last = product(nc, banks[b][:, :], (xh[:, k, tokens], xl[:, k, tokens]),
                                           w.operand(j, slice(q * HALF, (q + 1) * HALF)), k == 0, k == KT - 1)
                        last.then_inc(piece_done, 1)

        @block.scalar
        def _(act):
            with act.Fori(0, n_chunks) as c:
                for j in range(U):
                    w.highs(act, U * c + j, j)

        @block.vector
        def _(dve):
            dve.sem_inc(bank_free, nb)

            def turn(c, final):
                for j in range(U):
                    if not (final and j == U - 1):
                        w.lows(dve, U * c + (j + 1), (j + 1) % U)
                if loads:
                    dve.wait_ge(extra, 16 * len(loads))
                for b in range(nb):
                    dve.wait_ge(piece_done, U * nb * c + (nb * (U + 1) + b + 1))
                    evac(c, b, banks[b]).then_inc(bank_free, 1)

            w.lows(dve, 0, 0)
            if n_chunks > 1:
                with dve.Fori(0, n_chunks - 1) as c:
                    turn(c, False)
            turn(n_chunks - 1, True)
    co.end_phase()


def decay_phase(co, act_t, w_alr, w_up, b_alpha, decay):
    nc = co.nc
    sem = lambda n: co.sem(f"decay_{n}")
    loaded, rank_full, rank_ready, gate_full = sem("loaded"), sem("rank_full"), sem("rank_ready"), sem("gate_full")
    gate_ready, log_ready, reset_ready, done, act_done = (sem("gate_ready"), sem("log_ready"), sem("reset_ready"),
                                                         sem("done"), sem("act_done"))
    split = sem("split")
    with ExitStack() as cx:
        wh = co.sb("decay_wh", [P, KT * P], F32R, ctx=cx)
        wl = co.sb("decay_wl", [P, KT * P], F32R, ctx=cx)
        wu = co.sb("decay_wu", [RANK, 2 * P], ctx=cx)
        ba = co.sb("decay_ba", [P, 2], ctx=cx)
        gate = co.sb("decay_gate", [P, 2, SEQ], ctx=cx)
        mag = co.sb("decay_mag", [P, 2, SEQ], ctx=cx)
        wa = gate[:, 0, :]
        rank_t = mag[0:RANK, 0, :]
        keep = co.sb("decay_keep", [P, SEQ], ctx=cx)
        pr = cx.enter_context(nc.psum_tensor("decay_pr", [P, SEQ], F32))
        pg = cx.enter_context(nc.psum_tensor("decay_pg", [P, 2, SEQ], F32))
        block = cx.enter_context(nc.Block())

        @block.sync
        def _(sp):
            for dst, src in ((wa, w_alr), (wu[:, :], w_up), (ba[:, :], b_alpha)):
                sp.dma_start(dst, src).then_inc(loaded, 16)

        @block.gpsimd
        def _(pool):
            co.clear_stale(pool)
            pool.memset(keep[:, :], 1.0).then_inc(reset_ready, 1)
            pool.wait_ge(reset_ready, 1)
            pool.memset(keep[:, :].rearrange("p (c t) -> p c t", t=CHUNK)[:, :, 0:1], 0.0).then_inc(reset_ready, 1)

        @block.tensor
        def _(pe):
            pe.wait_ge(split, 2)
            for h in range(2):
                for k in range(KT):
                    tile, cols = slice(k * P, (k + 1) * P), slice(h * HALF, (h + 1) * HALF)
                    last = product(nc, pr[:, cols], (wh[:, tile], wl[:, tile]),
                                   (act_t[0][:, k, cols], act_t[1][:, k, cols]), k == 0, k == KT - 1)
                last.then_inc(rank_full, 1)
            for h in range(2):
                pe.wait_ge(rank_ready, h + 1)
                for p in range(2):
                    last = nc.tensor.matmul(pg[:, p, h * HALF:(h + 1) * HALF], wu[:, p * P:(p + 1) * P],
                                            rank_t[:, h * HALF:(h + 1) * HALF], start=True, stop=True)
            last.then_inc(gate_full, 1)

        @block.scalar
        def _(act):
            act.preload_act_table_set(LN_EXP)
            link = Chain(act, act_done)
            act.wait_ge(loaded, 48)
            high(nc, wh[:, :], wa).then_inc(split, 1)
            for h in range(2):
                act.wait_ge(rank_full, h + 1)
                nc.scalar.activation(rank_t[:, h * HALF:(h + 1) * HALF], pr[0:RANK, h * HALF:(h + 1) * HALF],
                                     ACT.Copy).then_inc(rank_ready, 1)
            for p in range(2):
                act.wait_ge(gate_ready, p + 1)
                link(nc.scalar.activation(mag[:, p, :], gate[:, p, :], ACT.Abs))
                link(nc.scalar.activation(mag[:, p, :], mag[:, p, :], ACT.Exp, scale=-1.0))
                nc.scalar.activation(mag[:, p, :], mag[:, p, :], ACT.Ln, bias=1.0).then_inc(log_ready, 1)

        @block.vector
        def _(dve):
            link = Chain(dve, done)
            dve.wait_ge(split, 1)
            low(nc, wl[:, :], wa, wh[:, :]).then_inc(split, 1)
            dve.wait_ge(gate_full, 1)
            for p in range(2):
                link(nc.vector.tensor_scalar(gate[:, p, :], pg[:, p, :], ba[:, p:p + 1], None, ALU.add))
                dve.sem_inc(gate_ready, 1)
            for p in range(2):
                dve.wait_ge(log_ready, p + 1)
                link(nc.vector.scalar_tensor_tensor(gate[:, p, :], gate[:, p, :], 0.0, mag[:, p, :],
                                                    ALU.min, ALU.subtract))
                dve.wait_ge(reset_ready, 2)
                link(nc.vector.tensor_tensor_scan(decay[:, p, :], keep[:, :], gate[:, p, :], 0.0, ALU.mult, ALU.add))
    co.end_phase()


def gla_phase(co, feat, tok, decay, act_t, weights, out):
    nc = co.nc
    sem = lambda n: co.sem(f"gla_{n}")
    args, exps, operands, values = sem("args"), sem("exps"), sem("operands"), sem("values")
    scores, turned, turned_sb, masked = sem("scores"), sem("turned"), sem("turned_sb"), sem("masked")
    sums, state_ready, o_full, o_free = sem("sums"), sem("state_ready"), sem("o_full"), sem("o_free")
    done, act_done, consts = sem("done"), sem("act_done"), sem("consts")
    half_full, half_free = sem("half_full"), sem("half_free")
    NC = P // CHUNK
    HALVES = SEQ // HALF
    with ExitStack() as cx:
        w = Weights(co, "gla_w", cx, HALVES, half_full, raw_slots=2, U=2)
        eq = co.sb("gla_eq", [P, 2, P], ctx=cx)
        ei = co.sb("gla_ei", [P, 2, P], ctx=cx)
        ek = co.sb("gla_ek", [P, 2, NC, NSUB, CHUNK], ctx=cx)
        ed = co.sb("gla_ed", [P, 2, P], ctx=cx)
        end = co.sb("gla_end", [P, 2, 2, NC], ctx=cx)
        qh = co.sb("gla_qh", [P, 2, 2, P], ctx=cx)
        qi = co.sb("gla_qi", [P, 2, 2, P], ctx=cx)
        kh = co.sb("gla_kh", [P, 2, 2, NC, NSUB, CHUNK], ctx=cx)
        kd = co.sb("gla_kd", [P, 2, 2, P], ctx=cx)
        kt = co.sb("gla_kt", [P, 2, 2 * P], ctx=cx)
        at = co.sb("gla_at", [P, 2, GLA_HEADS, P], ctx=cx)
        vb = co.sb("gla_vb", [P, 2, HALF], ctx=cx)
        state = co.sb("gla_state", [P, 2, 2, GLA_DV], ctx=cx)
        mask = co.sb("gla_mask", [P, 2, CHUNK], ctx=cx)
        ps = lambda n, shape: cx.enter_context(nc.psum_tensor(n, shape, F32))
        pa = [ps(f"gla_pa{j}", [P, 2, CHUNK]) for j in range(2)]
        po = [ps(f"gla_po{j}", [P, 2, GLA_DV]) for j in range(2)]
        pst = [ps(f"gla_pst{j}", [P, 2, GLA_DV]) for j in range(2)]
        pk = ps("gla_pk", [P, 2 * P])
        half_bank = ps("gla_half", [P, HALF])
        block = cx.enter_context(nc.Block())

        def blk(ap, b):
            return ap[:, :, ds(b * P, P)]

        @block.sync
        def _(sp):
            w.loads(sp, NB, lambda m: weights[ds(m, 1)].rearrange("o p c -> p (o c)"))

        @block.gpsimd
        def _(pool):
            co.clear_stale(pool)
            pool.memset(state[:, :, :, :], 0.0).then_inc(state_ready, 1)
            pool.memset(at[:, :, :, :], 0.0).then_inc(consts, 1)
            pool.memset(mask[:, :, :], 1.0).then_inc(consts, 1)
            pool.wait_ge(consts, 2)
            pool.affine_select(out=mask[:, :, :], in_=mask[:, :, :], compare_op=ALU.is_ge, fill=0.0, base=0,
                               pattern=[[CHUNK, 2], [1, CHUNK]], channel_multiplier=-1).then_inc(consts, 1)

            def value(b, s):
                pool.tensor_copy(vb[:, s, :], tok[:, T_VG, ds(b, 1), :].rearrange("p o c -> p (o c)")).then_inc(values, 1)

            value(0, 0)
            value(1, 1)
            with pool.Fori(0, NB // 2 - 1) as i:
                for s in range(2):
                    pool.wait_ge(sums, 2 * (2 * i + s + 1))
                    value(2 * i + 2 + s, s)

        @block.vector
        def _(dve):
            link = Chain(dve, done)

            def empty(n, h):
                dve.wait_ge(half_full, HALVES * n + (2 * HALVES + h + 1))
                nc.vector.tensor_copy(out[:, ds(n, 1), h * HALF:(h + 1) * HALF].rearrange("p o t -> p (o t)"),
                                      half_bank[:, :]).then_inc(half_free, 1)

            def operand(b, s):
                link.restart()
                bb = blk(decay, b)
                mid = bb.rearrange("p a (u s) -> p a u s", s=SUB)
                nc.vector.tensor_tensor(eq[:, :, :].rearrange("p a (u s) -> p a u s", s=SUB), mid,
                                        mid[:, :, :, SUB // 2 - 1:SUB // 2].broadcast_to([P, 2, P // SUB, SUB]),
                                        ALU.subtract).then_inc(args, 1)
                for a in range(2):
                    row = decay[:, a, ds(b * P, P)].rearrange("p (c t) -> p c t", c=NC)
                    ref = row.rearrange("p c (u s) -> p c u s", s=SUB)[:, :, :, SUB // 2 - 1:SUB // 2]
                    link(nc.vector.tensor_tensor(ek[:, a, :, :, :], ref.broadcast_to([P, NC, NSUB, CHUNK]),
                                                 row.unsqueeze(2).broadcast_to([P, NC, NSUB, CHUNK]), ALU.subtract))
                ekf = ek[:, :, :, :, :].rearrange("p a c u s -> p (a c u s)")
                nc.vector.tensor_scalar(ekf, ekf, EXP_CAP * TAU, None, ALU.min).then_inc(args, 1)
                row = bb.rearrange("p a (c t) -> p a c t", c=NC)
                nc.vector.tensor_tensor(ed[:, :, :].rearrange("p a (c t) -> p a c t", c=NC),
                                        row[:, :, :, CHUNK - 1:CHUNK].broadcast_to([P, 2, NC, CHUNK]), row,
                                        ALU.subtract).then_inc(args, 1)
                q, k = blk(feat[:, F_QG:F_QG + 2, :], b), blk(feat[:, F_KG:F_KG + 2, :], b)
                dve.wait_ge(exps, 4 * b + 2)
                nc.vector.scalar_tensor_tensor(qh[:, s, :, :], q, GLA_DK ** -0.5, eq[:, :, :], ALU.mult, ALU.mult)\
                    .then_inc(done, 1)
                nc.vector.scalar_tensor_tensor(qi[:, s, :, :], q, GLA_DK ** -0.5, ei[:, :, :], ALU.mult, ALU.mult)\
                    .then_inc(done, 1)
                dve.wait_ge(exps, 4 * b + 3)
                for a in range(2):
                    kk = feat[:, F_KG + a, ds(b * P, P)].rearrange("p (c t) -> p c t", c=NC)
                    nc.vector.tensor_tensor(kh[:, s, a, :, :, :], ek[:, a, :, :, :],
                                            kk.unsqueeze(2).broadcast_to([P, NC, NSUB, CHUNK]), ALU.mult).then_inc(done, 1)
                dve.wait_ge(exps, 4 * b + 4)
                link.n += 4
                link(nc.vector.tensor_tensor(kd[:, s, :, :], ed[:, :, :], k, ALU.mult))
                dve.sem_inc(operands, 1)
                w.lows(dve, b, s)

            def attend(b, s):
                link.restart()
                dve.wait_ge(scores, b + 1)
                dve.wait_ge(consts, 3)
                atv = at[:, s, :, :].rearrange("p (a h) t -> p a h t", h=2)
                for h in range(2):
                    for c in range(NC):
                        rows = slice(c * CHUNK, (c + 1) * CHUNK)
                        link(nc.vector.tensor_tensor(
                            atv[rows, :, h, c * CHUNK:(c + 1) * CHUNK], pa[h][rows, :, :],
                            mask[rows, c:c + 1, :].broadcast_to([CHUNK, 2, CHUNK]), ALU.mult))
                dve.sem_inc(masked, 1)
                empty(b, 0)
                for c in range(NC):
                    if c:
                        empty(b, 1)
                    dve.wait_ge(sums, 2 * b + c + 1)
                    for a in range(2):
                        link(nc.vector.scalar_tensor_tensor(state[:, 1 - c, a, :], state[:, c, a, :],
                                                            end[:, s, a, c:c + 1], pst[c][:, a, :], ALU.mult, ALU.add))
                    dve.sem_inc(state_ready, 1)

            dve.sem_inc(half_free, 1)
            steps(dve, operand, attend)

        @block.scalar
        def _(act):
            def operand(b, s):
                w.highs(act, b, s)
                act.wait_ge(args, 3 * b + 1)
                nc.scalar.activation(eq[:, :, :], eq[:, :, :], ACT.Exp, scale=1 / TAU).then_inc(exps, 1)
                nc.scalar.activation(ei[:, :, :], blk(decay, b), ACT.Exp, scale=1 / TAU).then_inc(exps, 1)
                act.wait_ge(args, 3 * b + 2)
                ekf = ek[:, :, :, :, :].rearrange("p a c u s -> p (a c u s)")
                nc.scalar.activation(ekf, ekf, ACT.Exp, scale=1 / TAU).then_inc(exps, 1)
                act.wait_ge(args, 3 * b + 3)
                row = blk(decay, b).rearrange("p a (c t) -> p a c t", c=NC)
                nc.scalar.activation(end[:, s, :, :], row[:, :, :, CHUNK - 1], ACT.Exp, scale=1 / TAU).then_inc(act_done, 1)
                act.wait_ge(act_done, b + 1)
                nc.scalar.activation(ed[:, :, :], ed[:, :, :], ACT.Exp, scale=1 / TAU).then_inc(exps, 1)

            def attend(b, s):
                act.wait_ge(turned, b + 1)
                nc.scalar.activation(kt[:, s, :], pk[:, :], ACT.Copy).then_inc(turned_sb, 1)
                act.wait_ge(o_full, b + 1)
                ov = tok[:, T_VG, ds(b, 1), :].rearrange("p o (a h e) -> p (o a) h e", a=2, h=2)
                for h in range(2):
                    nc.scalar.activation(ov[:, :, h, :], po[h][:, :, :], ACT.Copy).then_inc(o_free, 1)

            act.sem_inc(o_free, 2)
            steps(act, operand, attend)

        @block.tensor
        def _(pe):
            def half(n, s, h):
                pe.wait_ge(w.ready, n + 1)
                pe.wait_ge(half_free, HALVES * n + (h + 1))
                cols = slice(h * HALF, (h + 1) * HALF)
                for k in range(KT):
                    last = product(nc, half_bank[:, :], w.operand(s, slice(k * P, (k + 1) * P)),
                                   (act_t[0][:, k, cols], act_t[1][:, k, cols]), k == 0, k == KT - 1)
                last.then_inc(half_full, 1)

            pe.sem_inc(half_full, 2 * HALVES)
            with pe.Fori(0, NB // 2) as i:
                for s in range(2):
                    b = 2 * i + s
                    wait_alone(co, pe, operands, b + 1)
                    for h in range(2):
                        feats = slice(h * CHUNK, (h + 1) * CHUNK)
                        for a in range(2):
                            for c in range(NC):
                                for u in range(NSUB):
                                    last = nc.tensor.matmul(
                                        pa[h][c * CHUNK:(c + 1) * CHUNK, a, u * SUB:(u + 1) * SUB],
                                        kh[feats, s, a, c, u, :],
                                        qh[feats, s, a, c * CHUNK + u * SUB:c * CHUNK + (u + 1) * SUB],
                                        start=True, stop=True)
                    last.then_inc(scores, 1)
                    for a in range(2):
                        last = nc.tensor.transpose(pk[:, a * P:(a + 1) * P], kd[:, s, a, :], co.ident[:, :])
                    last.then_inc(turned, 1)
                    half(b, s, 0)
                    pe.wait_ge(masked, b + 1)
                    pe.wait_ge(values, b + 1)
                    pe.wait_ge(o_free, 2 * b + 2)
                    for h in range(2):
                        for a in range(2):
                            nc.tensor.matmul(po[h][:, a, :], at[:, s, 2 * a + h, :],
                                             vb[:, s, (2 * a + h) * GLA_DV:(2 * a + h + 1) * GLA_DV],
                                             start=(a == 0), stop=False, skip_group_check=True)
                    for c in range(NC):
                        rows = slice(c * CHUNK, (c + 1) * CHUNK)
                        if c:
                            half(b, s, 1)
                        wait_alone(co, pe, state_ready, 2 * b + c + 1)
                        for h in range(2):
                            feats = slice(h * CHUNK, (h + 1) * CHUNK)
                            for a in range(2):
                                last = nc.tensor.matmul(po[h][rows, a, :], qi[feats, s, a, rows], state[feats, c, a, :],
                                                        start=False, stop=(c == NC - 1), skip_group_check=True)
                        if c == NC - 1:
                            last.then_inc(o_full, 1)
                        if c == 0:
                            wait_alone(co, pe, turned_sb, b + 1)
                        for h in range(2):
                            feats = slice(h * CHUNK, (h + 1) * CHUNK)
                            for a in range(2):
                                hd = 2 * a + h
                                last = nc.tensor.matmul(pst[c][feats, a, :], kt[rows, s, hd * GLA_DK:(hd + 1) * GLA_DK],
                                                        vb[rows, s, hd * GLA_DV:(hd + 1) * GLA_DV], start=True, stop=True)
                        last.then_inc(sums, 1)
    co.end_phase()


def gla_norm_phase(co, heads, tok, gain, mix_t):
    nc = co.nc
    sem = lambda n: co.sem(f"glanorm_{n}")
    var_ready, guess_ready, gate_ready, scaled, turned, done, act_done, loaded, free = (
        sem("var_ready"), sem("guess_ready"), sem("gate_ready"), sem("scaled"), sem("turned"), sem("done"),
        sem("act_done"), sem("loaded"), sem("free"))
    hi_ready = sem("hi_ready")
    R = NB * GLA_HEADS
    with ExitStack() as cx:
        small = co.sb("glanorm_small", [P, 4, R], ctx=cx)
        g = co.sb("glanorm_gain", [P, 1], ctx=cx)
        sq = co.sb("glanorm_sq", [P, NB, HALF], ctx=cx)
        pt = [cx.enter_context(nc.psum_tensor(f"glanorm_pt{j}", [P, GLA_HEADS, P], F32)) for j in range(2)]
        block = cx.enter_context(nc.Block())
        ms, var, tmp, rstd = (small[:, j, :] for j in range(4))
        o = heads[:, 0, :, :]
        gate = tok[:, T_OG - 1, :, :]
        rows = lambda ap: ap.rearrange("p b (h e) -> p (b h) e", e=GLA_DV)

        @block.gpsimd
        def _(pool):
            co.clear_stale(pool)

        @block.sync
        def _(sp):
            sp.dma_start(g[:, :], gain).then_inc(loaded, 16)

        @block.vector
        def _(dve):
            link = Chain(dve, done)
            link(nc.vector.tensor_tensor(sq[:, :, :], o, o, ALU.mult))
            link(nc.vector.tensor_reduce(ms, rows(sq[:, :, :]), AX, ALU.add))
            nc.vector.tensor_scalar(var, ms, 1.0 / GLA_DV, EPS, ALU.mult, ALU.add).then_inc(var_ready, 1)
            dve.wait_ge(guess_ready, 1)
            rstd_steps(link, nc, ms, var, tmp, rstd)

            def part(b):
                dve.wait_ge(hi_ready, b + 1)
                hi = mix_t[0][:, 0:GLA_HEADS, b * P:(b + 1) * P]
                nc.vector.scalar_tensor_tensor(mix_t[1][:, 0:GLA_HEADS, b * P:(b + 1) * P], pt[b % 2][:, :, :], g[:, 0:1],
                                               hi.bitcast(F32), ALU.mult, ALU.subtract).then_inc(free, 1)

            for b in range(NB):
                ob = heads[:, 0, b, :].rearrange("p (h e) -> p h e", e=GLA_DV)
                r = small[:, 3, b * GLA_HEADS:(b + 1) * GLA_HEADS].unsqueeze(2).broadcast_to([P, GLA_HEADS, GLA_DV])
                link(nc.vector.tensor_tensor(ob, ob, r, ALU.mult))
                dve.wait_ge(gate_ready, 1)
                nc.vector.tensor_tensor(ob, ob, tok[:, T_OG - 1, b, :].rearrange("p (h e) -> p h e", e=GLA_DV),
                                        ALU.mult).then_inc(scaled, 1)
                if b:
                    part(b - 1)
            part(NB - 1)

        @block.tensor
        def _(pe):
            for b in range(NB):
                pe.wait_ge(scaled, b + 1)
                if b >= 2:
                    pe.wait_ge(free, b - 1)
                for h in range(GLA_HEADS):
                    last = nc.tensor.transpose(pt[b % 2][:, h, :], heads[:, 0, b, h * P:(h + 1) * P], co.ident[:, :])
                last.then_inc(turned, 1)

        @block.scalar
        def _(act):
            act.preload_act_table_set(LN_EXP)
            link = Chain(act, act_done)
            act.wait_ge(var_ready, 1)
            link(nc.scalar.activation(tmp, var, ACT.Ln))
            nc.scalar.activation(rstd, tmp, ACT.Exp, scale=-0.5).then_inc(guess_ready, 1)
            nc.scalar.activation(gate, gate, ACT.Silu).then_inc(gate_ready, 1)
            act.wait_ge(loaded, 16)
            for b in range(NB):
                act.wait_ge(turned, b + 1)
                nc.scalar.activation(mix_t[0][:, 0:GLA_HEADS, b * P:(b + 1) * P], pt[b % 2][:, :, :], ACT.Copy,
                                     scale=g[:, 0:1]).then_inc(hi_ready, 1)
    co.end_phase()


def stick_phase(co, feat, tok, mix_t, negtri, negone):
    nc = co.nc
    sem = lambda n: co.sem(f"stick_{n}")
    z_full, logs, sp_ready, sp_masked, carry_ready, r_full, a_ready, a_masked, pv_done, o_free = (
        sem(n) for n in ("z_full", "logs", "sp_ready", "sp_masked", "carry_ready", "r_full", "a_ready",
                         "a_masked", "pv_done", "o_free"))
    q_ready, kv_ready, act_done, hi_ready = sem("q_ready"), sem("kv_ready"), sem("act_done"), sem("hi_ready")
    NH = SEQ // HALF
    QB = HALF // P
    S = 4

    work = [(h, th, j, max(0, j - QB * th) * P) for th in range(NH) for j in range(QB * th + QB - 1, -1, -1)
            for h in range(2)]
    N = len(work)
    diag = [j >= QB * th for _, th, j, _ in work]
    carries = [j > 0 for _, _, j, _ in work]
    last_of = [j == 0 for _, _, j, _ in work]
    adds = [0 if not c else (1 if not d else (2 if w[3] + P < HALF else 1)) for c, d, w in zip(carries, diag, work)]
    C = 2

    def upto(flags, n):
        return sum(flags[:n + 1]) if n >= -1 else -sum(flags[n + 1:])

    with ExitStack() as cx:
        qp = co.sb("stick_q", [P, SEQ], ctx=cx)
        kp = co.sb("stick_k", [P, SEQ], ctx=cx)
        vp = co.sb("stick_v", [P, NB, P], ctx=cx)
        t = co.sb("stick_t", [P, S, HALF], ctx=cx)
        sps = co.sb("stick_sp", [P, S, HALF], ctx=cx)
        aw = co.sb("stick_a", [P, S, HALF], ctx=cx)
        carry = co.sb("stick_carry", [P, 2, 2, HALF], ctx=cx)
        pz = [cx.enter_context(nc.psum_tensor(f"stick_pz{j}", [P, HALF], F32)) for j in range(S)]
        po = [[cx.enter_context(nc.psum_tensor(f"stick_po{h}{j}", [P, HALF], F32)) for j in range(NH)] for h in range(2)]
        block = cx.enter_context(nc.Block())

        @block.gpsimd
        def _(pool):
            co.clear_stale(pool)
            pool.sem_inc(carry_ready, C)
            with pool.Fori(0, SB_HEADS // 2) as pr:
                wait_alone(co, pool, pv_done, N * pr + S)
                pool.tensor_copy(kp[:, :], feat[:, ds(F_KS - F_QS + pr, 1), :].rearrange("p o t -> p (o t)")).then_inc(kv_ready, 1)
                pool.tensor_copy(vp[:, :, :], tok[:, T_VS - 1, :, ds(pr * P, P)]).then_inc(kv_ready, 1)

                def strict(ap, c0, done):
                    pool.affine_select(out=ap[:, c0:c0 + P], in_=ap[:, c0:c0 + P], compare_op=ALU.is_gt, fill=0.0,
                                       base=0, pattern=[[1, P]], channel_multiplier=-1).then_inc(done, 1)

                for m in range(N + 2):
                    if m < N:
                        h, th, j, c0 = work[m]
                        s = m % S
                        wait_alone(co, pool, sp_ready, N * pr + (m + 1 + S))
                        if diag[m]:
                            strict(sps[:, s, :], c0, sp_masked)
                        if carries[m]:
                            k = QB * th + QB - 1 - j
                            new, old = carry[:, h, k % 2, :], carry[:, h, (k + 1) % 2, :]
                            wait_alone(co, pool, r_full, N * pr + (m - 2 + 1 + S))
                            if diag[m]:
                                wait_alone(co, pool, sp_masked, sum(diag) * pr + (upto(diag, m)))
                            c1 = c0 + P if diag[m] else c0
                            if c1 < HALF:
                                pool.wait_ge(carry_ready, sum(adds) * pr + (upto(adds, m - 2) + C))
                                ins = pool.tensor_tensor(new[:, c1:], old[:, c1:], sps[:, s, c1:], ALU.add)
                                ins.then_inc(carry_ready, 1)
                            if diag[m]:
                                pool.tensor_copy(new[:, c0:c1], sps[:, s, c0:c1]).then_inc(carry_ready, 1)
                    if m >= 2 and diag[m - 2]:
                        wait_alone(co, pool, a_ready, N * pr + (m - 2 + 1 + S))
                        strict(aw[:, (m - 2) % S, :], work[m - 2][3], a_masked)

        @block.scalar
        def _(act):
            link = Chain(act, act_done)
            act.preload_act_table_set(LN_EXP)
            act.sem_inc(a_ready, S)
            with act.Fori(0, SB_HEADS // 2) as pr:
                act.wait_ge(pv_done, N * pr + S)
                nc.scalar.activation(qp[:, :], feat[:, ds(pr, 1), :].rearrange("p o t -> p (o t)"), ACT.Copy,
                                     scale=SB_DH ** -0.5).then_inc(q_ready, 1)
                link.restart()
                for m in range(N + 2):
                    if m < N:
                        c0, s = work[m][3], m % S
                        act.wait_ge(z_full, N * pr + (m + 1))
                        act.wait_ge(sp_ready, N * pr + (m - S + 1 + S))
                        link(nc.scalar.activation(t[:, s, c0:], pz[s][:, c0:], ACT.Abs))
                        link(nc.scalar.activation(t[:, s, c0:], t[:, s, c0:], ACT.Exp, scale=-1.0))
                        nc.scalar.activation(t[:, s, c0:], t[:, s, c0:], ACT.Ln, bias=1.0).then_inc(logs, 1)
                    if m >= 2:
                        n = m - 2
                        c0, s = work[n][3], n % S
                        act.wait_ge(pv_done, N * pr + (n - S + 1 + S))
                        act.wait_ge(r_full, N * pr + (n + 1 + S))
                        nc.scalar.activation(aw[:, s, c0:], pz[s][:, c0:], ACT.Exp).then_inc(a_ready, 1)

        @block.vector
        def _(dve):
            dve.sem_inc(sp_ready, S)
            dve.sem_inc(o_free, 2 * NH)
            with dve.Fori(0, SB_HEADS // 2) as pr:
                for m in range(N + 5):
                    if m < N:
                        c0, s = work[m][3], m % S
                        dve.wait_ge(r_full, N * pr + (m - S + 1 + S))
                        dve.wait_ge(carry_ready, sum(adds) * pr + (upto(adds, m - S) + C))
                        dve.wait_ge(logs, N * pr + (m + 1))
                        nc.vector.scalar_tensor_tensor(sps[:, s, c0:], pz[s][:, c0:], 0.0, t[:, s, c0:],
                                                       ALU.max, ALU.add).then_inc(sp_ready, 1)
                    n = m - 4
                    if 0 <= n < N and last_of[n]:
                        h, th, _, _ = work[n]
                        rows = slice(h * SB_DH, (h + 1) * SB_DH)
                        dve.wait_ge(pv_done, N * pr + (n + 1 + S))
                        hi, lo = (m[rows, ds(GLA_HEADS + pr, 1), th * HALF:(th + 1) * HALF].rearrange("p o t -> p (o t)")
                                  for m in mix_t)
                        nc.vector.tensor_copy(hi, po[h][th][rows, :]).then_inc(hi_ready, 1)
                        dve.wait_ge(hi_ready, 2 * NH * pr + (2 * th + h + 1))
                        low(nc, lo, po[h][th][rows, :], hi).then_inc(o_free, 1)

        @block.tensor
        def _(pe):
            pe.sem_inc(r_full, S)
            pe.sem_inc(pv_done, S)
            with pe.Fori(0, SB_HEADS // 2) as pr:
                wait_alone(co, pe, q_ready, pr + 1)
                wait_alone(co, pe, kv_ready, 2 * pr + 2)
                for m in range(N + 4):
                    if m < N:
                        h, th, j, c0 = work[m]
                        rows = slice(h * SB_DH, (h + 1) * SB_DH)
                        wait_alone(co, pe, a_ready, N * pr + (m - S + 1 + S))
                        nc.tensor.matmul(pz[m % S][:, c0:], kp[rows, j * P:(j + 1) * P],
                                         qp[rows, th * HALF + c0:(th + 1) * HALF], start=True, stop=False,
                                         skip_group_check=True).then_inc(z_full, 1)
                    n = m - 2
                    if 0 <= n < N:
                        h, th, j, c0 = work[n]
                        s = n % S
                        if diag[n]:
                            pe.wait_ge(sp_masked, sum(diag) * pr + (upto(diag, n)))
                        else:
                            pe.wait_ge(sp_ready, N * pr + (n + 1 + S))
                        k = QB * th + QB - 1 - j
                        c1 = c0 + P if diag[n] else c0
                        last = nc.tensor.matmul(pz[s][:, c0:], negtri[:, :], sps[:, s, c0:], start=False,
                                                stop=(c1 == HALF), skip_group_check=True)
                        if c1 < HALF:
                            pe.wait_ge(carry_ready, sum(adds) * pr + (upto(adds, n - 2) + C))
                            last = nc.tensor.matmul(pz[s][:, c1:], negone[:, :], carry[:, h, (k + 1) % 2, c1:],
                                                    start=False, stop=True, skip_group_check=True)
                        last.then_inc(r_full, 1)
                    n = m - 4
                    if 0 <= n < N:
                        h, th, j, c0 = work[n]
                        rows = slice(h * SB_DH, (h + 1) * SB_DH)
                        first = j == QB * th + QB - 1
                        if first:
                            wait_alone(co, pe, o_free, 2 * NH * pr + (2 * th + h + 1))
                        if diag[n]:
                            pe.wait_ge(a_masked, sum(diag) * pr + (upto(diag, n)))
                        else:
                            pe.wait_ge(a_ready, N * pr + (n + 1 + S))
                        nc.tensor.matmul(po[h][th][rows, c0:], vp[:, j, rows], aw[:, n % S, c0:], start=first,
                                         stop=(j == 0), skip_group_check=True).then_inc(pv_done, 1)
    co.end_phase()


def memory_attention_phase(co, q_t, k_t, v, out_t):
    nc = co.nc
    sem = lambda n: co.sem(f"mem_{n}")
    q_ready, s_full, max_ready, probs, normed, turned, turned_sb, o_full, o_taken = (
        sem(n) for n in ("q_ready", "s_full", "max_ready", "probs", "normed", "turned", "turned_sb", "o_full", "o_taken"))
    done = sem("done")
    scale = MEM_DH ** -0.5
    HD = MEM_DH // P
    with ExitStack() as cx:
        qb = co.sb("mem_qb", [P, 2, KT, P], ctx=cx)
        pr = co.sb("mem_probs", [P, 2, MEM_HEADS, MEM], ctx=cx)
        prt = co.sb("mem_probs_t", [P, MEM_HEADS * MB, P], ctx=cx)
        stat = co.sb("mem_stat", [P, 2, 4, MEM_HEADS], ctx=cx)
        ps = [cx.enter_context(nc.psum_tensor(f"mem_ps{j}", [P, MEM_HEADS, MEM], F32)) for j in range(2)]
        pt = cx.enter_context(nc.psum_tensor("mem_pt", [P, MEM_HEADS * MB, P], F32))
        po = cx.enter_context(nc.psum_tensor("mem_po", [P, KT, P], F32))
        block = cx.enter_context(nc.Block())

        @block.gpsimd
        def _(pool):
            co.clear_stale(pool)

        def each(eng, body):
            with eng.Fori(0, NB // 2 - 1) as i:
                for s in range(2):
                    body(2 * i + s, s, True)
            for s in range(2):
                body(NB - 2 + s, s, False)

        @block.scalar
        def _(act):
            def queries(b, s):
                act.wait_ge(s_full, b + 1)
                nc.scalar.activation(qb[:, s, :, :], q_t[:, :, ds(b * P, P)], ACT.Copy).then_inc(q_ready, 1)

            def exps(b, s):
                act.wait_ge(max_ready, b + 1)
                for h in range(MEM_HEADS):
                    nc.scalar.activation(pr[:, s, h, :], ps[s][:, h, :], ACT.Exp, bias=stat[:, s, 1, h:h + 1],
                                         scale=scale, accum_out=stat[:, s, 2, h:h + 1]).then_inc(probs, 1)

            def body(b, s, more):
                act.wait_ge(turned, b + 1)
                nc.scalar.activation(prt[:, :, :], pt[:, :, :], ACT.Copy).then_inc(turned_sb, 1)
                if more:
                    queries(b + 2, s)
                    exps(b + 2, s)

            for b in range(2):
                queries(b, b)
            for b in range(2):
                exps(b, b)
            each(act, body)

        @block.tensor
        def _(pe):
            pe.sem_inc(s_full, 2)

            def attend(b, s):
                pe.wait_ge(q_ready, b + 1)
                for h in range(MEM_HEADS):
                    for k in range(HD):
                        last = nc.tensor.matmul(ps[s][:, h, :], qb[:, s, HD * h + k, :], k_t[:, HD * h + k, :],
                                                start=(k == 0), stop=(k == HD - 1))
                last.then_inc(s_full, 1)

            def body(b, s, more):
                pe.wait_ge(normed, b + 1)
                for h in range(MEM_HEADS):
                    for m in range(MB):
                        last = nc.tensor.transpose(pt[:, MB * h + m, :], pr[:, s, h, m * P:(m + 1) * P], co.ident[:, :])
                last.then_inc(turned, 1)
                if more:
                    attend(b + 2, s)
                pe.wait_ge(turned_sb, b + 1)
                pe.wait_ge(o_taken, b + 1)
                for h in range(MEM_HEADS):
                    for k in range(HD):
                        f = HD * h + k
                        for m in range(MB):
                            last = nc.tensor.matmul(po[:, f, :], v[:, m, f * P:(f + 1) * P], prt[:, MB * h + m, :],
                                                    start=(m == 0), stop=(m == MB - 1))
                last.then_inc(o_full, 1)

            for b in range(2):
                attend(b, b)
            each(pe, body)

        @block.vector
        def _(dve):
            link = Chain(dve, done)
            dve.sem_inc(o_taken, 1)

            def maxima(b, s):
                mx, neg, tot, inv = (stat[:, s, j, :] for j in range(4))
                dve.wait_ge(s_full, b + (1 + 2))
                link(nc.vector.tensor_reduce(mx, ps[s][:, :, :], AX, ALU.max))
                nc.vector.tensor_scalar(neg, mx, -scale, None, ALU.mult).then_inc(max_ready, 1)

            def norms(b, s):
                mx, neg, tot, inv = (stat[:, s, j, :] for j in range(4))
                dve.wait_ge(probs, MEM_HEADS * (b + 1))
                link(nc.vector.reciprocal(inv, tot))
                nc.vector.tensor_tensor(pr[:, s, :, :], pr[:, s, :, :],
                                        inv.unsqueeze(2).broadcast_to([P, MEM_HEADS, MEM]), ALU.mult).then_inc(normed, 1)

            def body(b, s, more):
                link.restart()
                if more:
                    maxima(b + 2, s)
                dve.wait_ge(o_full, b + 1)
                hi, lo = (o[:, :, ds(b * P, P)] for o in out_t)
                link(nc.vector.tensor_copy(hi, po[:, :, :]))
                low(nc, lo, po[:, :, :], hi).then_inc(o_taken, 1)
                if more:
                    norms(b + 2, s)

            for b in range(2):
                maxima(b, b)
                norms(b, b)
            each(dve, body)
    co.end_phase()


def key_scores_phase(co, act_t, weights, sub_keys, scores):
    nc = co.nc
    sem = lambda n: co.sem(f"keys_{n}")
    NT = 2 * PH
    keys_landed, q_full, q_sb, s_full, s_taken = (sem(n) for n in ("keys_landed", "q_full", "q_sb", "s_full", "s_taken"))
    S = 2
    xh, xl = act_t
    with ExitStack() as cx:
        w = Weights(co, "keys", cx, 1, q_full, raw_slots=2)
        U = w.U
        sk = co.sb("keys_sk", [P, NT, P], ctx=cx)
        qt = co.sb("keys_qt", [P, S, SEQ], ctx=cx)
        pq = [cx.enter_context(nc.psum_tensor(f"keys_pq{j}", [P, SEQ], F32)) for j in range(S)]
        pss = [cx.enter_context(nc.psum_tensor(f"keys_ps{j}", [P, NB, P], F32)) for j in range(S)]
        block = cx.enter_context(nc.Block())

        @block.gpsimd
        def _(pool):
            co.clear_stale(pool)

        @block.sync
        def _(sp):
            w.loads(sp, NT, lambda m: weights[ds(m, 1)].rearrange("o p c -> p (o c)"),
                    lambda: sp.dma_start(sk[:, :, :], sub_keys).then_inc(keys_landed, 16))

        @block.tensor
        def _(pe):
            pe.sem_inc(s_full, S)
            pe.sem_inc(q_full, S)

            def project(n, j):
                pe.wait_ge(w.ready, n + 1)
                pe.wait_ge(q_sb, n + 1)
                for h in range(SEQ // HALF):
                    cols = slice(h * HALF, (h + 1) * HALF)
                    for k in range(KT):
                        last = product(nc, pq[j % S][:, cols], w.operand(j, slice(k * P, (k + 1) * P)),
                                       (xh[:, k, cols], xl[:, k, cols]), k == 0, k == KT - 1)
                last.then_inc(q_full, 1)

            def products(n, j):
                pe.wait_ge(q_sb, n + (1 + S))
                pe.wait_ge(s_taken, n + 1)
                for b in range(NB):
                    last = nc.tensor.matmul(pss[j % S][:, b, :], qt[:, j % S, b * P:(b + 1) * P],
                                            sk[:, ds(n, 1), :].rearrange("p o c -> p (o c)"), start=True, stop=True)
                last.then_inc(s_full, 1)

            pe.wait_ge(keys_landed, 16)
            ahead(pe, NT, U, project, products)

        def two_ahead(eng, split, take):
            split(0, 0)
            ahead(eng, NT - U, U, lambda n, j: split(n + 1, (j + 1) % U), take)
            split(NT - U + 1, 1)
            for j in range(U):
                if j + 2 < U:
                    split(NT - U + j + 2, j + 2)
                take(NT - U + j, j)

        @block.scalar
        def _(act):
            act.sem_inc(q_sb, S)

            def take(n, j):
                act.wait_ge(q_full, n + (1 + S))
                act.wait_ge(s_full, n + 1)
                nc.scalar.activation(qt[:, j % S, :], pq[j % S][:, :], ACT.Copy).then_inc(q_sb, 1)

            two_ahead(act, lambda n, j: w.highs(act, n, j), take)

        @block.vector
        def _(dve):
            dve.sem_inc(s_taken, S)

            def take(n, j):
                dve.wait_ge(s_full, n + (1 + S))
                nc.vector.tensor_copy(scores[:, :, ds(n, 1), :].rearrange("p b o c -> p (b o) c"),
                                      pss[j % S][:, :, :]).then_inc(s_taken, 1)

            two_ahead(dve, lambda n, j: w.lows(dve, n, j), take)
    co.end_phase()


def expert_phase(co, scores, rstd, uv, g_ffn, g_final, out):
    nc = co.nc
    sem = lambda n: co.sem(f"expert_{n}")
    G = NB * PH
    ROWS = PB = 8
    DG = 4
    E = 2 * D
    landed = [sem(f"landed{j}") for j in range(ROWS)]
    (gains_landed, iota_ready, s_ready, best_ready, exp_ready, index_ready, gate_ready, dots, diag_ready, row_used,
     acc_taken, var_ready, guess_ready, out_ready, stored, done, act_done, dot_done) = (
        sem(n) for n in ("gains_landed", "iota_ready", "s_ready", "best_ready", "exp_ready", "index_ready", "gate_ready",
                         "dots", "diag_ready", "row_used", "acc_taken", "var_ready", "guess_ready", "out_ready",
                         "stored", "done", "act_done", "dot_done"))
    with ExitStack() as cx:
        sb = lambda n, shape, dt=F32: co.sb(f"expert_{n}", shape, dt, ctx=cx)
        ring = sb("rows", [P, ROWS, E])
        rows = [ring[:, j, :] for j in range(ROWS)]
        gf, gl = sb("gffn", [P, D]), sb("gfinal", [P, D])
        xn, hb, ob = sb("xn", [P, D]), sb("hb", [P, D]), sb("ob", [P, D])
        s_in = sb("s_in", [P, 2, 2, NKEYS])
        s_rest = sb("s_rest", [P, NKEYS])
        top = sb("top", [P, 2, TOPK])
        top_i = sb("top_i", [P, 2, TOPK], U32)
        top_f = sb("top_f", [P, 2, TOPK])
        cand = sb("cand", [P, TOPK, TOPK])
        cand_rest = sb("cand_rest", [P, TOPK, TOPK])
        best = sb("best", [P, 2, TOPK])
        best_j = sb("best_j", [P, TOPK], U32)
        pos = sb("pos", [P, 2, TOPK], U32)
        pos_f = sb("pos_f", [P, 2, TOPK])
        iota = sb("iota", [P, TOPK])
        hot = sb("hot", [P, 2, TOPK, TOPK])
        picked = sb("picked", [P, 2, TOPK])
        index = sb("index", [P, 2, TOPK], U32)
        gate = sb("gate", [P, 2, TOPK])
        small = sb("small", [P, 6])
        small2 = sb("small2", [P, 4])
        dot = sb("dot", [P, 2, TOPK])
        wt = sb("wt", [P, 2, 2, TOPK])
        dg = sb("dg", [P, DG, P])
        acc = cx.enter_context(nc.psum_tensor("expert_acc", [P, D], F32))
        junk = cx.enter_context(nc.psum_tensor("expert_junk", [P, D], F32))
        block = cx.enter_context(nc.Block())
        groups = scores.rearrange("p b (h c) n -> p (b h) (c n)", c=2)

        def over_groups(eng, group, before=None, after=None):
            with eng.Fori(0, NB) as b:
                if before:
                    before(b)
                with eng.Fori(0, PH // 2) as i:
                    for s in range(2):
                        group(PH * b + 2 * i + s, s)
                if after:
                    after(b)

        @block.sync
        def _(sp):
            sp.dma_start(gf[:, :], g_ffn.broadcast_to([P, D])).then_inc(gains_landed, 16)
            sp.dma_start(gl[:, :], g_final.broadcast_to([P, D])).then_inc(gains_landed, 16)
            sp.sem_inc(stored, 16)
            with sp.Fori(0, NB) as b:
                wait_alone(co, sp, out_ready, b + 1)
                sp.dma_start(out[ds(b, 1)].rearrange("o p d -> p (o d)"), ob[:, :]).then_inc(stored, 16)
                wait_alone(co, sp, stored, 16 * b + 32)

        @block.gpsimd
        def _(pool):
            co.clear_stale(pool)
            pool.iota(iota[:, :], pattern=[[1, TOPK]], base=0, channel_multiplier=0,
                      allow_small_or_imprecise_dtypes=True).then_inc(iota_ready, 1)

            def group(g, s):
                wait_alone(co, pool, index_ready, g + 1)
                for r in range(TOPK):
                    wait_alone(co, pool, row_used, TOPK * g + r + 1)
                    pool.indirect_dma_start(
                        out=rows[r % ROWS], out_offset=None, in_=uv,
                        in_offset=bass.IndirectOffsetOnAxis(ap=index[:, s, r:r + 1], axis=0),
                        bounds_check=NKEYS * NKEYS - 1, oob_is_err=False).then_inc(landed[r % ROWS], 16)

            over_groups(pool, group)

        @block.vector
        def _(dve):
            link = Chain(dve, done)
            LOWEST = -3.0e38

            def top16(value, index_out, values, rest, flat=lambda x: x):
                for e in range(2):
                    part = slice(8 * e, 8 * e + 8)
                    src = values if e == 0 else rest
                    link(nc.vector.max(value[:, part], src))
                    link(nc.vector.max_index(index_out[:, part], value[:, part], src))
                    if e == 0:
                        link(nc.vector.match_replace(rest, value[:, part], src, LOWEST))

            def select(g, s):
                link.restart()
                wait_alone(co, dve, s_ready, g + 1)
                for c in range(2):
                    top16(top[:, c, :], top_i[:, c, :], s_in[:, s, c, :], s_rest[:, :])
                link(nc.vector.tensor_copy(top_f[:, :, :], top_i[:, :, :]))
                link(nc.vector.tensor_tensor(cand[:, :, :], top[:, 0, :].unsqueeze(2).broadcast_to([P, TOPK, TOPK]),
                                             top[:, 1, :].unsqueeze(1).broadcast_to([P, TOPK, TOPK]), ALU.add))
                flat = lambda x: x[:, :, :].rearrange("p a b -> p (a b)")
                top16(best[:, s, :], best_j[:, :], flat(cand), flat(cand_rest))
                link(nc.vector.tensor_scalar(small[:, s:s + 1], best[:, s, 0:1], -1.0, None, ALU.mult))
                dve.sem_inc(best_ready, 1)
                link(nc.vector.tensor_scalar(pos[:, 0, :], best_j[:, :], 4, None, ALU.logical_shift_right))
                link(nc.vector.tensor_scalar(pos[:, 1, :], best_j[:, :], TOPK - 1, None, ALU.bitwise_and))
                link(nc.vector.tensor_copy(pos_f[:, :, :], pos[:, :, :]))
                for c in range(2):
                    link(nc.vector.tensor_tensor(hot[:, c, :, :], pos_f[:, c, :].unsqueeze(2).broadcast_to([P, TOPK, TOPK]),
                                                 iota[:, :].unsqueeze(1).broadcast_to([P, TOPK, TOPK]), ALU.is_equal))
                    link(nc.vector.tensor_tensor(hot[:, c, :, :], hot[:, c, :, :],
                                                 top_f[:, c, :].unsqueeze(1).broadcast_to([P, TOPK, TOPK]), ALU.mult))
                link(nc.vector.tensor_reduce(picked[:, :, :], hot[:, :, :, :], AX, ALU.add))
                link(nc.vector.scalar_tensor_tensor(index[:, s, :], picked[:, 0, :], float(NKEYS), picked[:, 1, :],
                                                    ALU.mult, ALU.add))
                dve.sem_inc(index_ready, 1)
                dve.wait_ge(exp_ready, g + 1)
                link(nc.vector.reciprocal(small[:, 4 + s:5 + s], small[:, 2 + s:3 + s]))
                link(nc.vector.tensor_scalar(gate[:, s, :], best[:, s, :], small[:, 4 + s:5 + s], None, ALU.mult))
                dve.sem_inc(gate_ready, 1)

            def group(g, s):
                select(g + 1, 1 - s)
                for r in range(TOPK):
                    dve.wait_ge(landed[r % ROWS], 16 * (TOPK // ROWS * g + r // ROWS + 1))
                    link(nc.vector.tensor_tensor_reduce(junk[:, :], rows[r % ROWS][:, 0:D], xn[:, :], 1.0, 0.0,
                                                        ALU.mult, ALU.add, dot[:, s, r:r + 1]))
                    dve.sem_inc(dots, 1)

            def before(b):
                link.restart()
                link(nc.vector.scalar_tensor_tensor(xn[:, :], co.H[:, ds(b, 1), :].rearrange("p o d -> p (o d)"),
                                                    rstd[:, ds(b, 1)], gf[:, :], ALU.mult, ALU.mult))

            def after(b):
                link.restart()
                dve.wait_ge(row_used, TOPK * PH * (b + 1) + ROWS)
                link(nc.vector.tensor_copy(hb[:, :], acc[:, :]))
                dve.sem_inc(acc_taken, 1)
                ms, var, tmp, y = (small2[:, j:j + 1] for j in range(4))
                link(nc.vector.tensor_tensor_reduce(junk[:, :], hb[:, :], hb[:, :], 1.0, 0.0, ALU.mult, ALU.add, ms))
                nc.vector.tensor_scalar(var, ms, 1.0 / D, EPS, ALU.mult, ALU.add).then_inc(var_ready, 1)
                dve.wait_ge(guess_ready, b + 1)
                rstd_steps(link, nc, ms, var, tmp, y)
                dve.wait_ge(stored, 16 * b + 16)
                nc.vector.scalar_tensor_tensor(ob[:, :], hb[:, :], y, gl[:, :], ALU.mult, ALU.mult).then_inc(out_ready, 1)

            dve.sem_inc(acc_taken, 1)
            dve.wait_ge(iota_ready, 1)
            dve.wait_ge(gains_landed, 32)
            select(0, 0)
            over_groups(dve, group, before, after)

        @block.scalar
        def _(act):
            link = Chain(act, act_done)

            def scores_in(g, s):
                nc.scalar.activation(s_in[:, s, :, :].rearrange("p c n -> p (c n)"),
                                     groups[:, ds(g % G, 1), :].rearrange("p o n -> p (o n)"), ACT.Copy).then_inc(s_ready, 1)

            def exps(g, s):
                act.wait_ge(best_ready, g + 1)
                link(nc.scalar.activation(best[:, s, :], best[:, s, :], ACT.Exp, bias=small[:, s:s + 1],
                                          accum_out=small[:, 2 + s:3 + s]))
                act.sem_inc(exp_ready, 1)

            def group(g, s):
                link.restart()
                act.wait_ge(index_ready, g + 1)
                scores_in(g + 2, s)
                exps(g + 1, 1 - s)
                act.wait_ge(gate_ready, g + 1)
                for r in range(TOPK):
                    act.wait_ge(dots, TOPK * g + r + 1)
                    link(nc.scalar.activation(wt[:, s, 0, r:r + 1], dot[:, s, r:r + 1], ACT.Gelu))
                    link(nc.scalar.activation(wt[:, s, 1, r:r + 1], wt[:, s, 0, r:r + 1], ACT.Copy,
                                              scale=gate[:, s, r:r + 1]))
                    act.wait_ge(row_used, TOPK * g + r + 1 + ROWS - DG)
                    nc.scalar.activation(dg[:, r % DG, :], co.ident[:, :], ACT.Copy,
                                         scale=wt[:, s, 1, r:r + 1]).then_inc(diag_ready, 1)

            def after(b):
                act.preload_act_table_set(LN_EXP)
                link.restart()
                act.wait_ge(var_ready, b + 1)
                link(nc.scalar.activation(small2[:, 2:3], small2[:, 1:2], ACT.Ln))
                nc.scalar.activation(small2[:, 3:4], small2[:, 2:3], ACT.Exp, scale=-0.5).then_inc(guess_ready, 1)

            scores_in(0, 0)
            scores_in(1, 1)
            exps(0, 0)
            over_groups(act, group, None, after)

        @block.tensor
        def _(pe):
            pe.sem_inc(row_used, ROWS)

            def before(b):
                pe.wait_ge(acc_taken, b + 1)
                for h in range(2):
                    nc.tensor.matmul(acc[:, h * HALF:(h + 1) * HALF], co.ident[:, :],
                                     co.H[:, ds(b, 1), h * HALF:(h + 1) * HALF].rearrange("p o d -> p (o d)"),
                                     start=True, stop=False, skip_group_check=True)

            def group(g, s):
                for r in range(TOPK):
                    pe.wait_ge(diag_ready, TOPK * g + r + 1)
                    for h in range(2):
                        last = nc.tensor.matmul(acc[:, h * HALF:(h + 1) * HALF], dg[:, r % DG, :],
                                                rows[r % ROWS][:, D + h * HALF:D + (h + 1) * HALF],
                                                start=False, stop=False, skip_group_check=True)
                    last.then_inc(row_used, 1)

            over_groups(pe, group, before)
    co.end_phase()


def program(nc, a, out):
    with ExitStack() as ctx:
        co = Core(nc, ctx)
        co.steps = ctx.enter_context(nc.semaphore("steps"))
        co.ident = co.sb("ident", [P, P])
        co.H = co.sb("H", [P, NB, D])
        gains = co.sb("gains", [P, 4, KT])
        rstd = co.sb("rstd", [P, NB])

        def halves(name, width, cx):
            return [co.sb(f"{name}_{part}", [P, KT, width], F32R, ctx=cx) for part in ("hi", "lo")]

        mix = ctx.enter_context(ExitStack())
        negtri, negone = co.sb("negtri", [P, P], ctx=mix), co.sb("negone", [P, P], ctx=mix)
        prep = ctx.enter_context(nc.semaphore("prep"))
        gl = ctx.enter_context(nc.semaphore("gl"))
        with nc.Block() as block:
            @block.gpsimd
            def _(pool):
                pool.memset(co.ident[:, :], 0.0).then_inc(prep, 1)
                pool.memset(negone[:, :], -1.0).then_inc(prep, 1)
                pool.memset(negtri[:, :], -1.0).then_inc(prep, 1)
                pool.wait_ge(prep, 3)
                pool.affine_select(out=negtri[:, :], in_=negtri[:, :], compare_op=ALU.is_ge, fill=0.0,
                                   base=0, pattern=[[-1, P]], channel_multiplier=1).then_inc(prep, 1)
                pool.affine_select(out=co.ident[:, :], in_=co.ident[:, :], compare_op=ALU.not_equal, fill=1.0,
                                   base=0, pattern=[[-1, P]], channel_multiplier=1).then_inc(prep, 1)
            @block.sync
            def _(sp):
                sp.dma_start(gains[:, :, :], a['gains'][:, :, :]).then_inc(gl, 16)
                sp.wait_ge(gl, 16)
        xv = a['x'].rearrange("(b p) d -> p b d", p=P)
        loads = [(co.H[:, 2 * j:2 * j + 2, :], xv[:, 2 * j:2 * j + 2, :]) for j in range(4)]
        with mix:
            x_t = halves("x_t", SEQ, mix)
            norm_phase(co, "mixnorm", co.H, NB, gains[:, 0, :], x_t, rstd[:, :], loads=loads)
            with ExitStack() as cx:
                def keep(dst):
                    return lambda c, b, bank: nc.vector.tensor_copy(dst[:, ds(c, 1), b, :].rearrange("p o c -> p (o c)"),
                                                                    bank[:, :])
                heads = co.sb("heads", [P, 1, NB, HALF], ctx=cx)
                token_gemm_phase(co, "glavalues", x_t, NB, a['w_tok'][0:4], 1, keep(heads))
                with ExitStack() as gl:
                    feat = co.sb("feat", [P, F_QS, SEQ], ctx=gl)
                    feature_gemm_phase(co, "glafeat", x_t, SEQ, a['w_feat'][0:F_QS], F_QS, feat)
                    decay = co.sb("decay", [P, 2, SEQ], ctx=gl)
                    decay_phase(co, x_t, a['w_alr'], a['w_up'], a['b_alpha'], decay)
                    gla_phase(co, feat, heads, decay, x_t, a['w_feat'][F_QS:NFEAT], co.H)
                tok = co.sb("tok", [P, NTOK - 1, NB, HALF], ctx=cx)
                token_gemm_phase(co, "mixtok", x_t, NB, a['w_tok'][4:4 * NTOK], NTOK - 1, keep(tok))
                gla_norm_phase(co, heads, tok, a['g_gla'], x_t)
                stick_phase(co, co.H, tok, x_t, negtri, negone)
            def add(c, b, bank):
                h = co.H[:, b, ds(c * HALF, HALF)]
                return nc.vector.tensor_tensor(h, h, bank[:, :], ALU.add)
            token_gemm_phase(co, "mixout", x_t, NB, a['w_out'], D // HALF, add, loads=loads)
        with ExitStack() as mem:
            x_t = halves("y_t", SEQ, mem)
            with ExitStack() as cx:
                q_t = co.sb("q_t", [P, KT, SEQ], ctx=cx)
                k_t = co.sb("k_t", [P, KT, MEM], ctx=cx)
                v_m = co.sb("v_m", [P, MB, D], ctx=cx)
                with ExitStack() as kv:
                    m_tok = co.sb("m_tok", [P, MB, D], ctx=kv)
                    m_t = halves("m_t", MEM, kv)
                    norm_phase(co, "memnorm", m_tok, MB, gains[:, 2, :], m_t, rstd[:, 0:MB],
                               loads=[(m_tok[:, :, :], a['mem'].rearrange("(b p) d -> p b d", p=P))])
                    feature_gemm_phase(co, "memk", m_t, MEM, a['w_mk'], KT, k_t)
                    token_gemm_phase(co, "memv", m_t, MB, a['w_mv'], D // HALF,
                                     lambda c, b, bank: nc.vector.tensor_copy(v_m[:, b, ds(c * HALF, HALF)], bank[:, :]))
                norm_phase(co, "qnorm", co.H, NB, gains[:, 1, :], x_t, rstd[:, :])
                feature_gemm_phase(co, "memq", x_t, SEQ, a['w_mq'], KT, q_t)
                memory_attention_phase(co, q_t, k_t, v_m, x_t)
            token_gemm_phase(co, "memout", x_t, NB, a['w_mo'], D // HALF, add)
        scores = co.sb("scores", [P, NB, 2 * PH, NKEYS])
        with ExitStack() as cx:
            x_t = halves("z_t", SEQ, cx)
            norm_phase(co, "ffnnorm", co.H, NB, gains[:, 3, :], x_t, rstd[:, :])
            key_scores_phase(co, x_t, a['w_pq'], a['sub_keys'], scores)
        expert_phase(co, scores[:, :, :, :], rstd, a['uv'], a['g_ffn'], a['g_final'],
                     out.rearrange("(b p) d -> b p d", p=P))


def kernel(**inputs):
    import numpy as np
    import concourse.bacc as bacc
    from concourse.bass_utils import run_bass_kernel_spmd

    i = {k: np.asarray(v) for k, v in inputs.items()}

    def by_feature(v):
        return v.reshape(-1, P).T

    def column_tiles(w, width):
        n, parts = w.shape[1] // width, width // P
        return w.reshape(parts, KT // parts, P, n, width).transpose(3, 0, 2, 1, 4).reshape(n * parts, P, KT * P)

    w_in = i["w_in"][0]
    bounds = np.cumsum([GLA_HEADS * GLA_DK, GLA_HEADS * GLA_DK, GLA_HEADS * GLA_DV, GLA_HEADS * GLA_DV, RANK,
                        SB_HEADS * SB_DH, SB_HEADS * SB_DH])
    qg, kg, vg, og, alr, qs, ks, vs = np.split(w_in, bounds, axis=1)
    w_mkv = i["w_mkv"][0]
    arrays = {
        "x": i["x"][0],
        "mem": i["mem"][0],
        "gains": np.stack([by_feature(i[n][0]) for n in ("g_mix", "g_mem_q", "g_mem_kv", "g_ffn")], axis=1),
        "w_feat": column_tiles(np.concatenate([qg, kg, qs, ks], axis=1), P),
        "w_tok": column_tiles(np.concatenate([vg, og, vs], axis=1), HALF),
        "w_alr": column_tiles(np.pad(alr, ((0, 0), (0, P - RANK))), P)[0],
        "w_up": i["w_alpha_up"][0],
        "b_alpha": by_feature(i["b_alpha"][0]),
        "g_gla": by_feature(i["g_gla_out"][0]),
        "w_out": column_tiles(i["w_out"][0], HALF),
        "w_mq": column_tiles(i["w_mq"][0], P),
        "w_mk": column_tiles(w_mkv[:, :D], P),
        "w_mv": column_tiles(w_mkv[:, D:], HALF),
        "w_mo": column_tiles(i["w_mo"][0], HALF),
        "w_pq": column_tiles(i["w_pq"][0], P),
        "sub_keys": i["sub_keys"][0].reshape(2 * PH, NKEYS, P).transpose(2, 0, 1),
        "uv": np.concatenate([i["peer_u"][0], i["peer_v"][0]], axis=1),
        "g_ffn": i["g_ffn"][0:1],
        "g_final": i["g_final"].reshape(1, D),
    }
    arrays = {f"in_{k}": np.ascontiguousarray(v) for k, v in arrays.items()}
    nc = bacc.Bacc("TRN2", target_bir_lowering=False, num_devices=1)
    a = {k[3:]: nc.dram_tensor(k, v.shape, mybir.dt.from_np(v.dtype), kind="ExternalInput").ap()
         for k, v in arrays.items()}
    out = nc.dram_tensor("out_0", (SEQ, D), F32, kind="ExternalOutput").ap()
    program(nc, a, out)
    r = run_bass_kernel_spmd(nc, [arrays], core_ids=[0])
    return r.results[0]["out_0"].reshape(1, SEQ, D)
```
